# Optimizing a Trainium2 kernel written in Bass

```python
import math
import jax, jax.numpy as jnp
from jax import lax
import numpy as np

D_MODEL = 1024
BATCH = 1
SEQ = 512
DEPTH = 1
DEC_BATCH = 8
DEC_SEQ = 8
PAST_LEN = 512
PAGE_SIZE = 128

DA_HEADS = 8
DA_DK = 64
DA_DV = 2 * DA_DK
DA_QK_W = DA_HEADS * 2 * DA_DK
DA_V_W = DA_HEADS * DA_DV
Q_BLOCK = 128
CHUNK = 128
SG_GROUPS = 8
SG_WIDTH = 1024
SG_GDIM = SG_WIDTH // SG_GROUPS
N_MEM = 256
MX_HEADS = 4
MX_DH = 256
MX_W = MX_HEADS * MX_DH
N_BUCKETS = 32
MAX_DISTANCE = 128
N_BRANCH = 3
BR_IN = DA_V_W + SG_WIDTH + MX_W
IN_W = 2 * DA_QK_W + DA_V_W + 2 * SG_WIDTH + MX_W + N_BRANCH * D_MODEL
D_FF = -(-8 * D_MODEL // (3 * 256)) * 256
RMS_EPS = 1e-6
NEG_INF = -1e30

kernel_name = "gated_parallel_diffattn_chunkgmlp_memxattn_step"

def _rmsnorm(x, g):
    xf = x.astype(jnp.float32)
    y = xf * lax.rsqrt(jnp.mean(jnp.square(xf), axis=-1, keepdims=True) + RMS_EPS)
    return (y * g.astype(jnp.float32)).astype(x.dtype)

def _t5_bucket(dist):
    n = jnp.maximum(dist, 0)
    max_exact = N_BUCKETS // 2
    nf = jnp.maximum(n, 1).astype(jnp.float32)
    large = max_exact + (jnp.log(nf / max_exact) / math.log(MAX_DISTANCE / max_exact)
                         * (N_BUCKETS - max_exact)).astype(jnp.int32)
    large = jnp.minimum(large, N_BUCKETS - 1)
    return jnp.where(n < max_exact, n, large)

def _diff_attn_core(q, k, v, q_pos, k_pos, rel_bias, lam, lam_init, subln_g):
    dist = q_pos[:, None] - k_pos[None, :]
    bias = jnp.transpose(rel_bias[_t5_bucket(dist)], (2, 0, 1)).astype(jnp.float32)
    s = jnp.einsum('bqhcd,bkhcd->bchqk', q, k, preferred_element_type=jnp.float32) * (DA_DK ** -0.5) + bias
    s = jnp.where(dist >= 0, s, NEG_INF)
    p = jax.nn.softmax(s, axis=-1)
    a = p[:, 0] - lam * p[:, 1]
    o = jnp.einsum('bhqk,bkhd->bqhd', a.astype(v.dtype), v)
    return _rmsnorm(o, subln_g) * (1.0 - lam_init)

def _da_prompt(q, k, v, rel_bias, lam, lam_init, subln_g):
    B, S = q.shape[0], q.shape[1]
    nb = S // Q_BLOCK
    pos = jnp.arange(S, dtype=jnp.int32)
    qb = jnp.moveaxis(q.reshape(B, nb, Q_BLOCK, DA_HEADS, 2, DA_DK), 1, 0)

    def blk(args):
        qi, pi = args
        return _diff_attn_core(qi, k, v, pi, pos, rel_bias, lam, lam_init, subln_g)

    ob = lax.map(blk, (qb, pos.reshape(nb, Q_BLOCK)))
    return jnp.moveaxis(ob, 0, 1).reshape(B, S, DA_HEADS, DA_DV)

def _da_sample(q, k, v, past_k, past_v, rel_bias, lam, lam_init, subln_g):
    T = q.shape[1]
    P = past_k.shape[1]
    k_all = jnp.concatenate([past_k.astype(k.dtype), k], axis=1)
    v_all = jnp.concatenate([past_v.astype(v.dtype), v], axis=1)
    q_pos = P + jnp.arange(T, dtype=jnp.int32)
    k_pos = jnp.arange(P + T, dtype=jnp.int32)
    return _diff_attn_core(q, k_all, v_all, q_pos, k_pos, rel_bias, lam, lam_init, subln_g)

def _spatial_gate(u, v, sg_norm, sg_w, sg_b):
    B, T = u.shape[0], u.shape[1]
    L = min(T, CHUNK)
    nc = T // L
    vn = _rmsnorm(v, sg_norm)
    vg = vn.reshape(B, nc, L, SG_GROUPS, SG_GDIM)
    causal = jnp.tril(jnp.ones((L, L), dtype=bool))
    w = jnp.where(causal, sg_w[:, :L, :L], 0.0).astype(v.dtype)
    mix = jnp.einsum('gts,bnsgd->bntgd', w, vg) + jnp.transpose(sg_b[:, :L])[None, None, :, :, None].astype(v.dtype)
    out = u.reshape(B, nc, L, SG_GROUPS, SG_GDIM) * mix
    return out.reshape(B, T, SG_WIDTH), vn

def _cross_attn(q, k, v):
    s = jnp.einsum('bqhd,bkhd->bhqk', q, k, preferred_element_type=jnp.float32) * (MX_DH ** -0.5)
    p = jax.nn.softmax(s, axis=-1)
    return jnp.einsum('bhqk,bkhd->bqhd', p.astype(v.dtype), v)

def _mem_kv(mem, g_mem, w_mem_kv):
    B = mem.shape[0]
    kv = (_rmsnorm(mem, g_mem) @ w_mem_kv).reshape(B, mem.shape[1], 2, MX_HEADS, MX_DH)
    return kv[:, :, 0], kv[:, :, 1]

def _layer(x, l, past_k, past_v, mem_k, mem_v, g_attn, w_in, da_lam, da_subln, rel_bias,
           sg_norm, sg_w, sg_b, w_branch, w_out, g_ffn, w_up, w_down):
    B, T = x.shape[0], x.shape[1]
    h = _rmsnorm(x, g_attn)
    z = h @ w_in
    sizes = (DA_QK_W, DA_QK_W, DA_V_W, SG_WIDTH, SG_WIDTH, MX_W, N_BRANCH * D_MODEL)
    offs = np.cumsum(sizes)[:-1].tolist()
    zq, zk, zv, zu, zs, zm, zg = jnp.split(z, offs, axis=-1)

    q = zq.reshape(B, T, DA_HEADS, 2, DA_DK)
    k = zk.reshape(B, T, DA_HEADS, 2, DA_DK)
    v = zv.reshape(B, T, DA_HEADS, DA_DV)
    lam_init = 0.8 - 0.6 * math.exp(-0.3 * l)
    lp = da_lam.astype(jnp.float32)
    lam = jnp.exp(jnp.sum(lp[0] * lp[1])) - jnp.exp(jnp.sum(lp[2] * lp[3])) + lam_init
    if past_k is None:
        o_da = _da_prompt(q, k, v, rel_bias, lam, lam_init, da_subln)
    else:
        o_da = _da_sample(q, k, v, past_k, past_v, rel_bias, lam, lam_init, da_subln)

    o_sg, vn = _spatial_gate(jax.nn.gelu(zu), jax.nn.gelu(zs), sg_norm, sg_w, sg_b)

    o_mx = _cross_attn(zm.reshape(B, T, MX_HEADS, MX_DH), mem_k, mem_v)

    gates = jax.nn.sigmoid(zg).reshape(B, T, N_BRANCH, D_MODEL)
    merged = (gates[:, :, 0] * (o_da.reshape(B, T, DA_V_W) @ w_branch[:DA_V_W])
              + gates[:, :, 1] * (o_sg @ w_branch[DA_V_W:DA_V_W + SG_WIDTH])
              + gates[:, :, 2] * (o_mx.reshape(B, T, MX_W) @ w_branch[DA_V_W + SG_WIDTH:]))
    x = x + merged @ w_out

    a, b = jnp.split(_rmsnorm(x, g_ffn) @ w_up, 2, axis=-1)
    x = x + (jax.nn.silu(a) * b) @ w_down
    return x, zk.reshape(B, T, DA_HEADS, 2 * DA_DK), v, vn

def setup_inputs(seed: int = 0) -> dict:
    key = jax.random.key(seed)
    ks = jax.random.split(key, 32)
    n_pages = PAST_LEN // PAGE_SIZE
    used = DEC_BATCH * n_pages
    n_pool = used + (-(-used // 4))
    f32 = jnp.float32

    def nrm(k, shape, scale=1.0):
        return jax.random.normal(k, shape, f32) * scale

    page_table = jax.random.permutation(ks[7], n_pool)[:used].reshape(DEC_BATCH, n_pages).astype(jnp.int32)
    return {
        "x_prompt": nrm(ks[0], (BATCH, SEQ, D_MODEL)),
        "x_sample": nrm(ks[1], (DEC_BATCH, DEC_SEQ, D_MODEL)),
        "mem_prompt": nrm(ks[2], (BATCH, N_MEM, D_MODEL)),
        "cache_da_k": nrm(ks[3], (DEPTH, n_pool, PAGE_SIZE, DA_HEADS, 2 * DA_DK)),
        "cache_da_v": nrm(ks[4], (DEPTH, n_pool, PAGE_SIZE, DA_HEADS, DA_DV)),
        "cache_mem_k": nrm(ks[5], (DEPTH, DEC_BATCH, N_MEM, MX_HEADS, MX_DH)),
        "cache_mem_v": nrm(ks[6], (DEPTH, DEC_BATCH, N_MEM, MX_HEADS, MX_DH)),
        "page_table": page_table,
        "g_attn": 1.0 + nrm(ks[8], (DEPTH, D_MODEL), 0.05),
        "w_in": nrm(ks[9], (DEPTH, D_MODEL, IN_W), D_MODEL ** -0.5),
        "da_lam": nrm(ks[10], (DEPTH, 4, DA_DK), 0.1),
        "da_subln": 1.0 + nrm(ks[11], (DEPTH, DA_DV), 0.05),
        "rel_bias": nrm(ks[12], (N_BUCKETS, DA_HEADS), 0.5),
        "sg_norm": 1.0 + nrm(ks[13], (DEPTH, SG_WIDTH), 0.05),
        "sg_w": nrm(ks[14], (DEPTH, SG_GROUPS, CHUNK, CHUNK), CHUNK ** -0.5),
        "sg_b": 1.0 + nrm(ks[15], (DEPTH, SG_GROUPS, CHUNK), 0.1),
        "g_mem": 1.0 + nrm(ks[16], (DEPTH, D_MODEL), 0.05),
        "w_mem_kv": nrm(ks[17], (DEPTH, D_MODEL, 2 * MX_W), D_MODEL ** -0.5),
        "w_branch": nrm(ks[18], (DEPTH, BR_IN, D_MODEL), (BR_IN // N_BRANCH) ** -0.5),
        "w_out": nrm(ks[19], (DEPTH, D_MODEL, D_MODEL), D_MODEL ** -0.5),
        "g_ffn": 1.0 + nrm(ks[20], (DEPTH, D_MODEL), 0.05),
        "w_up": nrm(ks[21], (DEPTH, D_MODEL, 2 * D_FF), D_MODEL ** -0.5),
        "w_down": nrm(ks[22], (DEPTH, D_FF, D_MODEL), D_FF ** -0.5),
        "g_final": 1.0 + nrm(ks[23], (D_MODEL,), 0.05),
    }

def reference(x_prompt, x_sample, mem_prompt, cache_da_k, cache_da_v, cache_mem_k, cache_mem_v,
              page_table, g_attn, w_in, da_lam, da_subln, rel_bias, sg_norm, sg_w, sg_b,
              g_mem, w_mem_kv, w_branch, w_out, g_ffn, w_up, w_down, g_final):
    xp, xs = x_prompt, x_sample
    dkp, dvp, dks, dvs, mkp, mvp, sgs = [], [], [], [], [], [], []
    for l in range(DEPTH):
        mk, mv = _mem_kv(mem_prompt, g_mem[l], w_mem_kv[l])
        xp, kp, vp, _ = _layer(xp, l, None, None, mk, mv, g_attn[l], w_in[l], da_lam[l], da_subln[l],
                               rel_bias, sg_norm[l], sg_w[l], sg_b[l], w_branch[l], w_out[l],
                               g_ffn[l], w_up[l], w_down[l])
        past_k = cache_da_k[l][page_table].reshape(DEC_BATCH, -1, DA_HEADS, 2, DA_DK)
        past_v = cache_da_v[l][page_table].reshape(DEC_BATCH, -1, DA_HEADS, DA_DV)
        xs, ksm, vsm, vns = _layer(xs, l, past_k, past_v, cache_mem_k[l], cache_mem_v[l], g_attn[l], w_in[l],
                                   da_lam[l], da_subln[l], rel_bias, sg_norm[l], sg_w[l], sg_b[l],
                                   w_branch[l], w_out[l], g_ffn[l], w_up[l], w_down[l])
        dkp.append(kp); dvp.append(vp); dks.append(ksm); dvs.append(vsm)
        mkp.append(mk); mvp.append(mv); sgs.append(vns)
    y_prompt = _rmsnorm(xp, g_final)
    y_sample = _rmsnorm(xs, g_final)
    return (y_prompt, y_sample, jnp.stack(dkp), jnp.stack(dvp), jnp.stack(dks), jnp.stack(dvs),
            jnp.stack(mkp), jnp.stack(mvp), jnp.stack(sgs))


_drawn_inputs = setup_inputs


def setup_inputs(seed=0):
    import zlib

    import numpy as np

    out = dict(_drawn_inputs(seed))
    spreads = {}
    factors = {}
    for name, (base, spread) in spreads.items():
        noise = np.random.default_rng([zlib.crc32(name.encode()), seed]).standard_normal(out[name].shape)
        drawn = base * np.exp(spread * noise) if base else spread * noise
        out[name] = __import__('jax').numpy.asarray(drawn.astype(out[name].dtype))
    for name, factor in factors.items():
        out[name] = (out[name] * factor).astype(out[name].dtype)
    return out
```

```python
from contextlib import ExitStack

import concourse.bass as bass
from concourse import mybir

F32 = mybir.dt.float32
F32R = mybir.dt.float32r
I32 = mybir.dt.int32
ALU = mybir.AluOpType
ACT = mybir.ActivationFunctionType
AX = mybir.AxisListType

P = 128
D = 1024
KT = D // P
SEQ = 512
NB, TS = 8, 8
NS = NB * TS
T = SEQ + NS
HT = T // 2
QT = SEQ // P
PAST, PAGE = 512, 128
PAGES = PAST // PAGE
KEYS = PAST + TS
HK = KEYS // 2
HEADS, DK, DV = 8, 64, 128
MEM, MXH, MXD = 256, 4, 256
MT = MEM // P
GROUPS = 8
DFF = 2816
FT = DFF // P
DOWN_K = (8, 8, 6)
EPS = 1e-6
LAM_INIT = 0.2
NEG = -1e30
BUCKETS = 32
REV = KEYS + P
HREV = REV // 2

STAGES = (("q", 8), ("k", 8), ("v", 8), ("da_branch", 16), ("s", 8), ("u", 8), ("sg_branch", 16),
          ("zm", 8), ("mk", 8), ("mv", 8), ("mx_branch", 16), ("w_out", 8), ("up", 2 * FT), ("down", 24))
FIRST = {}
PANELS = 0
for _name, _n in STAGES:
    FIRST[_name] = PANELS
    PANELS += _n

C_ID, C_ONE, C_COMB, C_M8, C_M4, C_C1, C_INVD, C_END = 0, 128, 256, 320, 328, 332, 333, 334
G_ATTN, G_MEM, G_FFN, G_FINAL, G_SUB, G_REL, G_LAM, G_END = 0, 8, 16, 24, 32, 33, 41, 297


def decoder_layer(nc, xT, memT, w_stream, page_table, cache_k, cache_v, mem_k, mem_v, consts,
                  bias_select, params, sg_norm, sg_bias, sg_wT,
                  yT, kT_out, v_out, vs_out, mkT_out, mv_out, vn_out):
    ctx = ExitStack()
    with ctx:
        base = (nc.sbuf_base + 63) // 64 * 64
        top = nc.sbuf_usable_end

        class Region:
            def __init__(self, at):
                self.at = at

            def take(self, name, shape, dtype=F32):
                size = 4
                for n in shape[1:]:
                    size *= n
                t = nc.alloc_sbuf_tensor_at(name, shape, dtype, offset=self.at)
                self.at += (size + 31) // 32 * 32
                assert self.at <= top, (name, self.at, top)
                return t

        whole = Region(base)
        w_raw = whole.take("w_raw", [P, 2, D])
        w_hi = whole.take("w_hi", [P, 2, D], F32R)
        w_lo = whole.take("w_lo", [P, 2, D], F32R)
        cst = whole.take("cst", [P, C_END])
        par = whole.take("par", [P, G_END])
        small = whole.take("small", [P, 104])
        pages = whole.take("pages", [1, NB * PAGES], I32)
        lam_w = whole.take("lam_w", [1, 2 * DK + 8])
        diag_at = whole.at
        diag = whole.take("diag", [P, 5, P])
        x_sb = whole.take("x_sb", [P, KT, T])
        h_at = whole.at
        h_hi = whole.take("h_hi", [P, KT, T], F32R)
        h_lo = whole.take("h_lo", [P, KT, T], F32R)
        o_at = whole.at
        o_hi = whole.take("o_hi", [P, KT, T], F32R)
        o_lo = whole.take("o_lo", [P, KT, T], F32R)
        merged_at = whole.at
        merged = whole.take("merged", [P, KT, T])
        z_at = whole.at

        tail = Region(top - 4 * 6 * T - 64)
        tail.at = tail.at // 32 * 32
        tail_at = tail.at
        ssum = tail.take("ssum", [P, T])
        square = tail.take("square", [P, T])
        rms_b = tail.take("rms_b", [P, T])
        scaled = tail.take("scaled", [P, 2, T])
        gate = tail.take("gate", [P, T])

        da = Region(merged_at)
        bias_s = da.take("bias_s", [P, KEYS])
        logit_s = da.take("logit_s", [P, 2, KEYS])
        q_blk = da.take("q_blk", [P, HEADS, P])
        coef_s = da.take("coef_s", [P, 64])
        aT_s = da.take("aT_s", [P, (PAGES + 1) * 64])
        b_sel = Region(da.at).take("b_sel", [BUCKETS + 1, REV])
        masked_s = da.take("masked_s", [64, D])
        o_s = da.take("o_s", [64, 2, DV])
        assert da.at <= z_at
        da = Region(z_at)
        qT = da.take("qT", [P, KT, T])
        kT = da.take("kT", [P, KT, T])
        v_nat = da.take("v_nat", [P, QT + 1, D])
        assert da.at <= tail_at, (da.at, tail_at)
        v_new = Region(tail_at).take("v_new", [P, D])
        turn = scaled
        da = Region(o_at)
        k_pg = da.take("k_pg", [P, HEADS, KEYS])
        v_pg = da.take("v_pg", [P, PAGES, D])
        rel_line = da.take("rel_line", [HEADS, REV])
        da = Region(o_at)
        bias_p = da.take("bias_p", [P, 2, SEQ])
        q_z = da.take("q_z", [P, 2, 2, SEQ])
        logit_p = da.take("logit_p", [P, 2, 2, SEQ])
        a_p = da.take("a_p", [P, 2, SEQ])
        aT_p = da.take("aT_p", [P, 2, SEQ])
        o_p = da.take("o_p", [P, 2, SEQ])
        assert da.at <= merged_at

        sg = Region(z_at)
        s_nat = sg.take("s_nat", [P, QT + 1, D])
        s_slot = sg.take("s_slot", [P, 2, QT + 1, P])
        uT = sg.take("uT", [P, KT, T])
        norm_b = sg.take("norm_b", [P, D])
        sgb_b = sg.take("sgb_b", [P, GROUPS, P])
        sg_w = sg.take("sg_w", [P, GROUPS, P])
        sg_ws = Region(diag_at).take("sg_ws", [NS, GROUPS, NS])
        mixed = scaled[:, 0, :]
        assert sg.at <= tail_at, (sg.at, tail_at)

        mx = Region(z_at)
        zmT = mx.take("zmT", [P, KT, T])
        kmT = mx.take("kmT", [P, KT, MEM])
        m_x = Region(mx.at).take("m_x", [P, KT, MEM])
        vm_nat = mx.take("vm_nat", [P, MT, D])
        mx2 = Region(mx.at)
        m_hi = mx.take("m_hi", [P, KT, MEM], F32R)
        m_lo = mx.take("m_lo", [P, KT, MEM], F32R)
        assert mx.at <= tail_at, (mx.at, tail_at)
        q_mb = mx2.take("q_mb", [P, 2, KT, 32])
        p_mb = mx2.take("p_mb", [32, 2, MEM])
        pT_mb = mx2.take("pT_mb", [P, 2, MT * 32])
        q_m = mx2.take("q_m", [P, 2, SEQ])
        v_m = mx2.take("v_m", [P, MT, MXD])
        mx3 = Region(mx2.at)
        p_m = mx2.take("p_m", [P, QT, MEM])
        pT_m = mx2.take("pT_m", [P, MT, SEQ])
        masked_m = mx3.take("masked_m", [32, D])
        o_m = mx3.take("o_m", [32, 2, MXD])
        assert mx2.at <= tail_at
        mx2 = Region(o_at)
        km_pg = mx2.take("km_pg", [P, 2, KT, MEM])
        vm_pg = mx2.take("vm_pg", [P, 2, MT, D])

        wo = Region(z_at)
        m2_hi = wo.take("m2_hi", [P, KT, T], F32R)
        m2_lo = wo.take("m2_lo", [P, KT, T], F32R)
        assert wo.at <= tail_at
        ff = Region(o_at)
        g_hi = ff.take("g_hi", [P, FT, T], F32R)
        g_lo = ff.take("g_lo", [P, FT, T], F32R)
        assert ff.at <= tail_at, (ff.at, tail_at)
        y_sb = Region(h_at).take("y_sb", [P, KT, T])
        acc = [ctx.enter_context(nc.psum_tensor(f"acc{u}", [P, 2, 512], F32)) for u in range(2)]
        ps4 = ctx.enter_context(nc.psum_tensor("ps4", [P, 4, 512], F32))

        def bank(n):
            return acc[n // 2][:, n % 2, :] if n < 4 else ps4[:, n - 4, :]

        def halves(x):
            return x.rearrange("p (c n) -> p c n", c=2)

        def acc_t(u):
            return acc[u][:, :, 0:HT]

        def view(ap, dims, skip=0):
            return bass.AP(tensor=ap.tensor, offset=ap.offset + skip, ap=[list(ap.ap[0])] + dims)

        def col(n, rows=P, w=1):
            return small[0:rows, n:n + w]

        ident = cst[:, C_ID:C_ID + P]

        N_STAT, N_RS, N_HALF, N_LAM, N_LAMS = 0, 5, 10, 15, 18
        S_MAX, S_NEG, S_SUM, S_RC, S_SS, S_ST, S_R = range(20, 27)
        P_MAX, P_NEG, P_SUM, P_RC, P_SS, P_ST, P_R = 28, 32, 36, 40, 44, 52, 56
        M_NEG, M_SUM, M_RC, MP_NEG, MP_SUM, MP_RC = 64, 66, 68, 70, 74, 78
        G_SS, G_ST, G_RS, N_SUBG = 82, 87, 92, 100

        def sem(name):
            return ctx.enter_context(nc.semaphore(name))

        def sems(name, n=2):
            return [sem(f"{name}{i}") for i in range(n)]

        w_loaded = sems("w_loaded")
        w_hi_done = sem("w_hi_done")
        w_lo_done = sem("w_lo_done")
        mm_done = sem("mm_done")
        acc_free = sems("acc_free")
        down_free = sems("down_free")
        x_loaded = sem("x_loaded")
        cst_loaded = sem("cst_loaded")
        mem_loaded = sem("mem_loaded")
        sg_loaded = sem("sg_loaded")
        sgs_loaded = sem("sgs_loaded")
        const_set = sem("const_set")
        waits_passed = sem("waits_passed")
        v_zero = sem("v_zero")
        subg_ready = sem("subg_ready")
        lam_dot = sem("lam_dot")
        lam_exp = sem("lam_exp")
        lam_diff = sem("lam_diff")
        lam_neg = sem("lam_neg")
        lam_mm = sem("lam_mm")
        lam_ready = sem("lam_ready")
        line_mm = sem("line_mm")
        line_ready = sem("line_ready")
        line_stored = sem("line_stored")
        bias_skewed = sem("bias_skewed")
        bias_s_loaded = sem("bias_s_loaded")
        squared = sem("squared")
        summed = sem("summed")
        stat_mm = sem("stat_mm")
        stat_ready = sem("stat_ready")
        stat_pow = sem("stat_pow")
        diag_ready = sem("diag_ready")
        bcast_mm = sem("bcast_mm")
        rms_ready = sem("rms_ready")
        n_scaled = sem("n_scaled")
        n_hi = sem("n_hi")
        n_lo = sem("n_lo")
        y_ready = sem("y_ready")
        turned = sem("turned")
        nat_done = sem("nat_done")
        o_hi_done = sem("o_hi_done")
        o_lo_done = sem("o_lo_done")
        merged_done = sem("merged_done")
        ffn_hi = sem("ffn_hi")
        ffn_lo = sem("ffn_lo")
        stored = sem("stored")
        vs_stored = sem("vs_stored")
        y_stored = sem("y_stored")
        k_loaded = sem("k_loaded")
        v_loaded = sem("v_loaded")
        s_q = sem("s_q")
        s_scores = sem("s_scores")
        s_logit = sem("s_logit")
        s_neg = sem("s_neg")
        s_exp = sem("s_exp")
        s_rc = sem("s_rc")
        s_coef = sem("s_coef")
        s_comb = sem("s_comb")
        s_aT = sem("s_aT")
        s_pv = sem("s_pv")
        s_masked = sem("s_masked")
        s_osum = sem("s_osum")
        s_oss = sem("s_oss")
        s_ost = sem("s_ost")
        s_orms = sem("s_orms")
        s_onorm = sem("s_onorm")
        s_oT = sem("s_oT")
        s_oout = sem("s_oout")
        p_bias = sems("p_bias")
        p_q = sem("p_q")
        p_zero = sem("p_zero")
        p_scores = sem("p_scores")
        p_logit = sem("p_logit")
        p_neg = sem("p_neg")
        p_exp = sem("p_exp")
        p_rc = sem("p_rc")
        p_a1 = sem("p_a1")
        p_a = sem("p_a")
        p_turn = sem("p_turn")
        p_aT = sem("p_aT")
        p_pv = sem("p_pv")
        p_oss = sem("p_oss")
        p_ost = sem("p_ost")
        p_orms = sem("p_orms")
        p_onorm = sem("p_onorm")
        p_oT = sem("p_oT")
        p_oout = sem("p_oout")
        g_ss = sem("g_ss")
        g_st = sem("g_st")
        g_rs = sem("g_rs")
        g_norm = sem("g_norm")
        g_wmask = sem("g_wmask")
        g_zero = sem("g_zero")
        g_slot = sem("g_slot")
        g_mix = sem("g_mix")
        g_bias = sem("g_bias")
        g_out = sem("g_out")
        km_loaded = sems("km_loaded")
        vm_loaded = sems("vm_loaded")
        m_zero = sem("m_zero")
        m_q = sem("m_q")
        m_scores = sem("m_scores")
        m_neg = sem("m_neg")
        m_exp = sem("m_exp")
        m_rc = sem("m_rc")
        m_p = sem("m_p")
        m_turn = sem("m_turn")
        m_pT = sem("m_pT")
        m_pv = sem("m_pv")
        m_masked = sem("m_masked")
        m_o = sem("m_o")
        m_oT = sem("m_oT")
        m_oout = sem("m_oout")
        c_q = sem("c_q")
        c_v = sem("c_v")
        c_scores = sem("c_scores")
        c_neg = sem("c_neg")
        c_exp = sem("c_exp")
        c_rc = sem("c_rc")
        c_p = sem("c_p")
        c_turn = sem("c_turn")
        c_pT = sem("c_pT")
        c_pv = sem("c_pv")
        c_oout = sem("c_oout")

        line_d = nc.dram_tensor("line_d", [HEADS, REV], F32, kind="Internal").ap()
        bias_sd = nc.dram_tensor("bias_sd", [HEADS, 2, TS, KEYS], F32, kind="Internal").ap()
        bias_pd = nc.dram_tensor("bias_pd", [HEADS, P, SEQ], F32, kind="Internal").ap()

        def wait(eng, s, value):
            if not isinstance(value, int) or value > 0:
                eng.wait_ge(s, value)

        def settle(eng, i):
            if not isinstance(i, int):
                eng.sem_inc(waits_passed, 1)

        def peeled(eng, n, body, first=1):
            for i in range(first):
                body(i)
            with eng.Fori(first, n) as i:
                body(i)

        def pairs(eng, body):
            body(0)
            with eng.Fori(1, HEADS // 2 - 1) as hp:
                body(hp)
            body(HEADS // 2 - 1, True)

        def all_evacuated(eng, stage):
            for u in range(2):
                eng.wait_ge(acc_free[u], FIRST[stage] // 2)

        block = ctx.enter_context(nc.Block())

        @block.sync
        def _(sp):
            def load_w(p, u):
                wait(sp, w_lo_done, p - 1)
                sp.dma_start(w_raw[:, u, :], w_stream[bass.ds(p, 1)].rearrange("a p n -> (a p) n"))\
                    .then_inc(w_loaded[u], 16)

            def stream(start, end):
                with sp.Fori(start // 2, end // 2) as i:
                    for u in range(2):
                        load_w(2 * i + u, u)

            def page_of(b):
                return [sp.value_load(pages[0:1, bass.ds(b * PAGES + j, 1)], min_val=0,
                                      max_val=cache_k.shape[0] - 1) for j in range(PAGES)]

            def key_pages(b, at):
                wait(sp, s_scores, b)
                for j in range(PAGES):
                    sp.dma_start(k_pg[:, :, j * PAGE:(j + 1) * PAGE],
                                 cache_k[bass.ds(at[j], 1)].rearrange("a p (h n) -> (a p) h n", h=HEADS))\
                        .then_inc(k_loaded, 16)

            def value_pages(b, at):
                wait(sp, s_pv, b)
                for j in range(PAGES):
                    sp.dma_start(v_pg[:, j, :], cache_v[bass.ds(at[j], 1)].rearrange("a p n -> (a p) n"))\
                        .then_inc(v_loaded, 16)

            def load_new_values(b):
                if isinstance(b, int):
                    sp.wait_ge(vs_stored, 16)
                sp.dma_start(v_new[0:TS, :], vs_out[bass.ds(b * TS, TS), :]).then_inc(v_loaded, 16)

            def load_keys(b):
                key_pages(b, page_of(b))

            def load_values(b):
                value_pages(b, page_of(b))
                load_new_values(b)

            def load_keys_values(bk, bv):
                at_k, at_v = page_of(bk), page_of(bv)
                key_pages(bk, at_k)
                value_pages(bv, at_v)
                load_new_values(bv)

            sp.dma_start(x_sb[:, :, :], xT.rearrange("(k p) n -> p k n", p=P)).then_inc(x_loaded, 16)
            sp.dma_start(cst[:, :], consts).then_inc(cst_loaded, 16)
            sp.dma_start(par[:, :], params).then_inc(cst_loaded, 16)
            sp.dma_start(b_sel[:, :], bias_select).then_inc(cst_loaded, 16)
            for u in range(2):
                load_w(u, u)
            sp.dma_start(pages[:, :], page_table).then_inc(cst_loaded, 16)
            sp.wait_ge(line_ready, 2)
            sp.dma_start(line_d, rel_line[:, :]).then_inc(line_stored, 16)
            sp.wait_ge(line_stored, 16)
            for c in range(2):
                sp.dma_start(bias_sd[:, c], bass.AP(tensor=line_d.tensor, offset=TS - 1,
                                                    ap=[[REV, HEADS], [-1, TS], [1, KEYS]]))\
                    .then_inc(bias_skewed, 16)
            sp.dma_start(bias_pd, bass.AP(tensor=line_d.tensor, offset=KEYS - 1 - (SEQ - P),
                                          ap=[[REV, HEADS], [-1, P], [1, SEQ]])).then_inc(bias_skewed, 16)
            stream(2, FIRST["k"])
            sp.wait_ge(bias_skewed, 48)
            sp.wait_ge(cst_loaded, 64)
            sp.dma_start(bias_s[:, :], bias_sd.rearrange("h c t k -> (h c t) k")).then_inc(bias_s_loaded, 16)
            stream(FIRST["k"], FIRST["v"])
            at = page_of(0)
            key_pages(0, at)
            value_pages(0, at)
            stream(FIRST["v"], FIRST["da_branch"] + 2)

            sp.wait_ge(v_zero, 1)
            load_new_values(0)
            load_keys(1)
            load_keys(2)
            with sp.Fori(3, NB) as b:
                load_keys_values(b, b - 2)
            load_values(NB - 2)
            load_values(NB - 1)
            sp.wait_ge(s_oout, NB)

            def load_bias(hp):
                for e in range(2):
                    wait(sp, p_logit, 4 * (2 * hp + e - 1))
                    sp.dma_start(bias_p[:, e, :], bias_pd[bass.ds(2 * hp + e, 1)].rearrange("a p n -> (a p) n"))\
                        .then_inc(p_bias[e], 16)

            peeled(sp, HEADS // 2, load_bias)
            stream(FIRST["da_branch"] + 2, FIRST["s"])
            sp.wait_ge(o_lo_done, KT)
            sp.wait_ge(stored, 32)
            sp.dma_start(norm_b[:, :], bass.AP(tensor=sg_norm.tensor, offset=0, ap=[[0, P], [1, D]])).then_inc(sg_loaded, 16)
            sp.dma_start(sgb_b[:, :, :], bass.AP(tensor=sg_bias.tensor, offset=0, ap=[[0, P], [P, GROUPS], [1, P]])).then_inc(sg_loaded, 16)
            sp.dma_start(sg_w[:, :, :], sg_wT).then_inc(sg_loaded, 16)
            sp.wait_ge(g_zero, 1)
            for b in range(NB):
                sp.dma_start(sg_ws[b * TS:(b + 1) * TS, :, b * TS:(b + 1) * TS], sg_wT[0:TS, :, 0:TS],
                             allow_slow_non_contiguous=True).then_inc(sgs_loaded, 16)
            stream(FIRST["s"], FIRST["zm"])
            sp.wait_ge(o_lo_done, 2 * KT)
            sp.dma_start(m_x[:, :, :], memT.rearrange("(k p) n -> p k n", p=P)).then_inc(mem_loaded, 16)
            stream(FIRST["zm"], FIRST["mk"])
            sp.wait_ge(mm_done, FIRST["zm"])

            def load_mem(i):
                for e in range(2):
                    b = 2 * i + e
                    wait(sp, m_scores, b - 1)
                    sp.dma_start(km_pg[:, e], mem_k[bass.ds(b, 1)].rearrange("a p (f m) -> (a p) f m", f=KT))\
                        .then_inc(km_loaded[e], 16)
                    wait(sp, m_pv, b - 1)
                    sp.dma_start(vm_pg[:, e], mem_v[bass.ds(b, 1)].rearrange("a (m p) n -> (a p) m n", p=P))\
                        .then_inc(vm_loaded[e], 16)

            load_mem(0)
            stream(FIRST["mk"], FIRST["mx_branch"] + 2)
            with sp.Fori(1, NB // 2) as i:
                load_mem(i)
            stream(FIRST["mx_branch"] + 2, PANELS)
            for k in range(KT):
                sp.wait_ge(y_ready, k + 1)
                sp.dma_start(yT[k * P:(k + 1) * P, :], y_sb[:, k, :]).then_inc(y_stored, 16)
            sp.wait_ge(y_stored, 16 * KT)
            sp.wait_ge(stored, 16 * 5)
            sp.wait_ge(vs_stored, 16)

        @block.scalar
        def _(act):
            def split_hi(p, u):
                act.wait_ge(w_loaded[u], 16 * (p // 2 + 1) if isinstance(p, int) else 8 * (p - u) + 16)
                wait(act, mm_done, p - 1)
                nc.scalar.activation(w_hi[:, u, :], w_raw[:, u, :], ACT.Copy).then_inc(w_hi_done, 1)

            def evacuate(p, u, out, func=ACT.Copy, scale=1.0, n=2):
                act.wait_ge(mm_done, p + 1)
                src = acc_t(u) if n == 2 else acc[u][:, 0, 0:MEM]
                nc.scalar.activation(out, src, func, scale=scale).then_inc(acc_free[u], 1)

            def norm_squares(x, n_cols, count):
                for k in range(KT):
                    wait(act, summed, count + k - 1)
                    out = (square if k % 2 == 0 else gate)[:, 0:n_cols]
                    nc.scalar.activation(out, x[:, k, :], ACT.Square).then_inc(squared, 1)

            def rms_out(count, n_cols):
                act.wait_ge(bcast_mm, count + 1)
                if n_cols == T:
                    nc.scalar.activation(rms_b[:, 0:SEQ], bank(5), ACT.Copy)
                    nc.scalar.activation(rms_b[:, SEQ:T], bank(6)[:, 0:NS], ACT.Copy).then_inc(rms_ready, 1)
                else:
                    nc.scalar.activation(rms_b[:, 0:MEM], bank(5)[:, 0:MEM], ACT.Copy).then_inc(rms_ready, 1)

            def norm_hi(hi, n_cols, count):
                for k in range(KT):
                    act.wait_ge(n_scaled, count + k + 1)
                    nc.scalar.activation(hi[:, k, :], scaled[:, k % 2, 0:n_cols], ACT.Copy).then_inc(n_hi, 1)

            def o_split(src, count):
                for k in range(KT):
                    nc.scalar.activation(o_hi[:, k, :], src[:, k, :], ACT.Copy).then_inc(o_hi_done, 1)

            act.wait_ge(x_loaded, 16)
            norm_squares(x_sb, T, 0)
            split_hi(0, 0)
            split_hi(1, 1)
            act.wait_ge(cst_loaded, 64)
            act.wait_ge(const_set, 2)
            nc.scalar.activation(col(N_SUBG), par[:, G_SUB:G_SUB + 1], ACT.Copy, scale=1.0 - LAM_INIT)\
                .then_inc(subg_ready, 1)
            act.wait_ge(lam_dot, 2)
            nc.scalar.activation(lam_w[0:1, 2 * DK + 2:2 * DK + 4], lam_w[0:1, 2 * DK:2 * DK + 2], ACT.Exp)\
                .then_inc(lam_exp, 1)
            act.wait_ge(line_mm, 1)
            nc.scalar.activation(rel_line[:, 0:HREV], bank(7)[0:HEADS, 0:HREV], ACT.Copy).then_inc(line_ready, 1)
            nc.scalar.activation(rel_line[:, HREV:REV], bank(3)[0:HEADS, 0:HREV], ACT.Copy).then_inc(line_ready, 1)
            rms_out(0, T)
            norm_hi(h_hi, T, 0)

            for stage, dst, scale in (("q", qT, DK ** -0.5), ("k", kT, 1.0)):
                with act.Fori(0, 4) as i:
                    for u in range(2):
                        p = FIRST[stage] + 2 * i + u
                        evacuate(p, u, halves(dst[:, bass.ds(2 * i + u, 1), :].rearrange("p a n -> p (a n)")),
                                 scale=scale)
                        split_hi(p + 2, u)

            def turning(stage, count, func=ACT.Copy, n=2):
                def body(i):
                    for u in range(2):
                        p = FIRST[stage] + 2 * i + u
                        wait(act, turned, count + 2 * i + u - 1)
                        evacuate(p, u, halves(turn[:, u, :]) if n == 2 else turn[:, u, 0:MEM], func, n=n)
                        split_hi(p + 2, u)
                peeled(act, 4, body)

            turning("v", 0)

            def s_output(b):
                act.wait_ge(s_oT, b + 1)
                nc.scalar.activation(qT[:, :, bass.ds(SEQ + b * TS, TS)],
                                     bank(6)[:, 0:64].rearrange("p (h t) -> p h t", h=HEADS), ACT.Copy,
                                     scale=col(N_SUBG)).then_inc(s_oout, 1)

            def s_square(b):
                act.wait_ge(s_osum, b + 1)
                nc.scalar.activation(rms_b[0:64, 0:DV], o_s[:, 0, :], ACT.Square,
                                     accum_out=col(S_SS, 64)).then_inc(s_oss, 1)

            def s_body(i):
                for e in range(2):
                    b = 2 * i + e
                    if not isinstance(b, int) or b >= 3:
                        s_output(b - 3)
                    act.wait_ge(s_neg, b + 1)
                    nc.scalar.activation(logit_s[:, e, :], logit_s[:, e, :], ACT.Exp, bias=col(S_NEG),
                                         accum_out=col(S_SUM)).then_inc(s_exp, 1)
                    if not isinstance(b, int) or b >= 2:
                        s_square(b - 2)

            peeled(act, NB // 2, s_body, 2)
            s_output(NB - 3)
            s_square(NB - 2)
            s_output(NB - 2)
            s_square(NB - 1)
            s_output(NB - 1)

            def p_body(hp0, last_pair=False):
                def exps(n):
                    hp, n = hp0 + n // 8, n % 8
                    m, w = n % 2, (n % 4 + 1) * P
                    act.wait_ge(p_neg, 8 * hp + n + 1)
                    for c in range(2):
                        last = nc.scalar.activation(logit_p[:, m, c, 0:w], logit_p[:, m, c, 0:w], ACT.Exp,
                                                    bias=col(P_NEG + 2 * m + c), accum_out=col(P_SUM + 2 * m + c))
                    last.then_inc(p_exp, 1)

                def turned_probs(n):
                    hp = hp0
                    m, w = n % 2, (n % 4 + 1) * P
                    act.wait_ge(p_turn, 8 * hp + n + 1)
                    wait(act, p_pv, 8 * hp + n - 1)
                    nc.scalar.activation(aT_p[:, m, 0:w], bank(2 + m)[:, 0:w], ACT.Copy).then_inc(p_aT, 1)

                def squares(e, hp):
                    act.wait_ge(p_pv, 8 * hp + 4 * e + 4)
                    for i in range(QT):
                        last = nc.scalar.activation(rms_b[:, i * DV:(i + 1) * DV], bank(e)[:, i * DV:(i + 1) * DV], ACT.Square,
                                                    accum_out=col(P_SS + 4 * e + i))
                    last.then_inc(p_oss, 1)

                def output(e, hp):
                    act.wait_ge(p_oT, 2 * hp + e + 1)
                    nc.scalar.activation(qT[:, bass.ds(2 * hp + e, 1), 0:SEQ].rearrange("p a n -> p (a n)"),
                                         bank(e), ACT.Copy, scale=col(N_SUBG)).then_inc(p_oout, 1)

                first_pair = isinstance(hp0, int) and hp0 == 0
                if first_pair:
                    exps(0)
                for n in range(8):
                    if n < 7 or not last_pair:
                        exps(n + 1)
                    if n == 1 and not first_pair:
                        squares(1, hp0 - 1)
                    if n == 4 and not first_pair:
                        output(1, hp0 - 1)
                    if n == 5:
                        squares(0, hp0)
                    if n == 7:
                        output(0, hp0)
                    turned_probs(n)
                if last_pair:
                    squares(1, hp0)
                    output(1, hp0)

            pairs(act, p_body)

            def branch(stage):
                def body(i):
                    p = FIRST[stage] + 2 * i
                    act.wait_ge(acc_free[1], FIRST[stage] // 2 + i)
                    evacuate(p, 0, halves(gate[:, :]), ACT.Sigmoid)
                    split_hi(p + 2, 0)
                    act.wait_ge(mm_done, p + 2)
                    split_hi(p + 3, 1)
                with act.Fori(0, KT) as i:
                    body(i)

            act.wait_ge(p_oout, HEADS)
            o_split(qT, 0)
            branch("da_branch")

            turning("s", KT, ACT.Gelu_apprx_tanh)
            act.wait_ge(nat_done, 2 * KT)
            for j in range(QT + 1):
                rows = P if j < QT else NS
                place = s_slot[:, :, :, :].rearrange("p a j d -> p (a j d)") if j == QT else \
                    uT[:, :, :].rearrange("p k n -> p (k n)")[:, j * D:(j + 1) * D]
                last = nc.scalar.activation(place[0:rows, 0:D], s_nat[0:rows, j, :], ACT.Square, accum_out=col(G_SS + j, rows))
            last.then_inc(g_ss, 1)
            act.wait_ge(g_ss, 1)
            with act.Fori(0, 4) as i:
                for u in range(2):
                    p = FIRST["u"] + 2 * i + u
                    evacuate(p, u, halves(uT[:, bass.ds(2 * i + u, 1), :].rearrange("p a n -> p (a n)")),
                             ACT.Gelu_apprx_tanh)
                    split_hi(p + 2, u)
            for k in range(KT):
                act.wait_ge(g_out, k + 1)
                nc.scalar.activation(o_hi[:, k, :], uT[:, k, :], ACT.Copy).then_inc(o_hi_done, 1)
            branch("sg_branch")

            act.wait_ge(stored, 48)
            act.wait_ge(mem_loaded, 16)
            act.wait_ge(acc_free[1], FIRST["zm"] // 2)
            norm_squares(m_x, MEM, KT)
            def zm_body(i):
                for u in range(2):
                    p = FIRST["zm"] + 2 * i + u
                    evacuate(p, u, halves(zmT[:, bass.ds(2 * i + u, 1), :].rearrange("p a n -> p (a n)")),
                             scale=MXD ** -0.5)
                    split_hi(p + 2, u)
            zm_body(0)
            zm_body(1)
            rms_out(1, MEM)
            norm_hi(m_hi, MEM, KT)
            with act.Fori(2, 4) as i:
                zm_body(i)
            with act.Fori(0, 4) as i:
                for u in range(2):
                    p = FIRST["mk"] + 2 * i + u
                    evacuate(p, u, kmT[:, bass.ds(2 * i + u, 1), :].rearrange("p a n -> p (a n)"), n=1)
                    split_hi(p + 2, u)
            turning("mv", 2 * KT, n=1)

            def m_output(b):
                act.wait_ge(m_oT, b + 1)
                out = zmT[:, :, bass.ds(SEQ + b * TS, TS)].rearrange("p (h f) t -> p f h t", f=2)
                for f in range(2):
                    last = nc.scalar.activation(out[:, f], bank(7)[:, f * 32:f * 32 + 32]
                                                .rearrange("p (h t) -> p h t", h=MXH), ACT.Copy)
                last.then_inc(m_oout, 1)

            def m_body(i):
                for e in range(2):
                    b = 2 * i + e
                    act.wait_ge(m_neg, b + 1)
                    nc.scalar.activation(p_mb[:, e, :], bank(4 + e)[0:32, 0:MEM], ACT.Exp,
                                         bias=col(M_NEG + e, 32), accum_out=col(M_SUM + e, 32)).then_inc(m_exp, 1)
                    if not isinstance(i, int):
                        m_output(b - 2)
                    act.wait_ge(m_turn, b + 1)
                    wait(act, m_pv, b - 1)
                    nc.scalar.activation(pT_mb[:, e, :], bank(6)[:, 0:MT * 32], ACT.Copy).then_inc(m_pT, 1)

            peeled(act, NB // 2, m_body)
            m_output(NB - 2)
            m_output(NB - 1)

            def c_output(h):
                act.wait_ge(c_pv, h + 1)
                for f in range(2):
                    last = nc.scalar.activation(zmT[:, bass.ds(2 * h + f, 1), 0:SEQ].rearrange("p a n -> p (a n)"),
                                                bank(f), ACT.Copy)
                last.then_inc(c_oout, 1)

            def c_body(h):
                act.wait_ge(c_neg, h + 1)
                wait(act, c_turn, h)
                for i in range(QT):
                    last = nc.scalar.activation(p_m[:, i, :], bank(4 + i // 2)[:, (i % 2) * MEM:(i % 2 + 1) * MEM],
                                                ACT.Exp, bias=col(MP_NEG + i), accum_out=col(MP_SUM + i))
                last.then_inc(c_exp, 1)
                if not isinstance(h, int):
                    c_output(h - 1)
                act.wait_ge(c_turn, h + 1)
                for m in range(MT):
                    last = nc.scalar.activation(pT_m[:, m, :], bank(6 + m), ACT.Copy)
                last.then_inc(c_pT, 1)

            peeled(act, MXH, c_body)
            c_output(MXH - 1)
            act.wait_ge(c_oout, MXH)
            o_split(zmT, 2 * KT)
            branch("mx_branch")

            act.wait_ge(stored, 80)
            act.wait_ge(merged_done, 2 * KT)
            for k in range(KT):
                nc.scalar.activation(m2_hi[:, k, :], merged[:, k, :], ACT.Copy).then_inc(o_hi_done, 1)

            def resid_square(n, count):
                wait(act, summed, n + 2 * KT)
                nc.scalar.activation(square[:, :], x_sb[:, bass.ds(n - count, 1), :].rearrange("p a n -> p (a n)"),
                                     ACT.Square).then_inc(squared, 1)

            with act.Fori(0, 4) as i:
                for u in range(2):
                    p = FIRST["w_out"] + 2 * i + u
                    act.wait_ge(mm_done, p + 1)
                    split_hi(p + 2, u)
                    act.wait_ge(acc_free[u], FIRST["w_out"] // 2 + i + 1)
                    resid_square(2 * i + u, 0)
            rms_out(2, T)
            norm_hi(h_hi, T, 2 * KT)

            with act.Fori(0, FT) as i:
                p = FIRST["up"] + 2 * i
                act.wait_ge(acc_free[1], FIRST["up"] // 2 + i)
                evacuate(p, 0, halves(gate[:, :]), ACT.Silu)
                split_hi(p + 2, 0)
                act.wait_ge(mm_done, p + 2)
                split_hi(p + 3, 1)
                act.wait_ge(acc_free[1], FIRST["up"] // 2 + i + 1)
                nc.scalar.activation(g_hi[:, bass.ds(i, 1), :].rearrange("p a n -> p (a n)"), scaled[:, 0, :],
                                     ACT.Copy).then_inc(ffn_hi, 1)

            def down_body(i):
                for f in range(2):
                    for c in range(3):
                        q = 3 * f + c
                        p = FIRST["down"] + 6 * i + q
                        if isinstance(i, int) and p + 2 >= PANELS:
                            continue
                        act.wait_ge(mm_done, p + 1)
                        split_hi(p + 2, q % 2)
                    act.wait_ge(down_free[f], i + 1)
                    resid_square(KT + 2 * i + f, KT)
            with act.Fori(0, 3) as i:
                down_body(i)
            down_body(3)
            rms_out(3, T)

        @block.vector
        def _(dve):
            def split_lo(p, u):
                dve.wait_ge(w_hi_done, p + 1)
                nc.vector.tensor_tensor(w_lo[:, u, :], w_raw[:, u, :], w_hi[:, u, :].bitcast(F32), ALU.subtract)\
                    .then_inc(w_lo_done, 1)

            def norm_stats(count, n_cols):
                nt = 5 if n_cols == T else 2
                dve.wait_ge(stat_mm, count + 1)
                nc.vector.tensor_scalar(col(N_STAT, w=nt), bank(4)[:, 0:nt], EPS, None, ALU.add)\
                    .then_inc(stat_ready, 1)
                dve.wait_ge(stat_pow, count + 1)
                for j in range(nt):
                    last = nc.vector.tensor_scalar(diag[:, j, :], ident, col(N_RS + j), None, ALU.mult)
                last.then_inc(diag_ready, 1)

            def norm_scale(x, gain, n_cols, count, n_rms):
                dve.wait_ge(rms_ready, n_rms)
                for k in range(KT):
                    wait(dve, n_lo, count + k - 1)
                    nc.vector.scalar_tensor_tensor(scaled[:, k % 2, 0:n_cols], x[:, k, :],
                                                   par[:, gain + k:gain + k + 1], rms_b[:, 0:n_cols],
                                                   ALU.mult, ALU.mult).then_inc(n_scaled, 1)

            dve.wait_ge(cst_loaded, 64)
            for c in range(2):
                nc.vector.tensor_tensor_reduce(out=lam_w[0:1, c * DK:(c + 1) * DK],
                                               in0=par[0:1, G_LAM + 2 * c * DK:G_LAM + (2 * c + 1) * DK],
                                               in1=par[0:1, G_LAM + (2 * c + 1) * DK:G_LAM + (2 * c + 2) * DK],
                                               scale=1.0, scalar=0.0, op0=ALU.mult, op1=ALU.add,
                                               accum_out=lam_w[0:1, 2 * DK + c:2 * DK + c + 1]).then_inc(lam_dot, 1)
            dve.wait_ge(lam_exp, 1)
            nc.vector.tensor_tensor(lam_w[0:1, 2 * DK + 4:2 * DK + 5], lam_w[0:1, 2 * DK + 3:2 * DK + 4],
                                    lam_w[0:1, 2 * DK + 2:2 * DK + 3], ALU.subtract).then_inc(lam_diff, 1)
            dve.wait_ge(lam_diff, 1)
            nc.vector.tensor_scalar(lam_w[0:1, 2 * DK + 5:2 * DK + 6], lam_w[0:1, 2 * DK + 4:2 * DK + 5],
                                    LAM_INIT, None, ALU.subtract).then_inc(lam_neg, 1)
            dve.wait_ge(lam_mm, 1)
            nc.vector.tensor_copy(col(N_LAM), bank(2)[:, 0:1]).then_inc(lam_ready, 1)
            dve.wait_ge(lam_ready, 1)
            nc.vector.tensor_scalar(col(N_LAMS), cst[:, C_C1:C_C1 + 1], col(N_LAM), None, ALU.mult)\
                .then_inc(lam_ready, 1)
            dve.wait_ge(lam_ready, 2)
            nc.vector.scalar_tensor_tensor(col(N_LAMS), cst[:, C_C1:C_C1 + 1], -1.0, col(N_LAMS), ALU.mult, ALU.add)\
                .then_inc(lam_ready, 1)
            dve.wait_ge(lam_ready, 3)
            nc.vector.tensor_scalar(col(N_LAMS), col(N_LAMS), 1.0, None, ALU.add).then_inc(lam_ready, 1)
            split_lo(0, 0)
            split_lo(1, 1)
            norm_stats(0, T)
            norm_scale(x_sb, G_ATTN, T, 0, 1)

            def lows(stage, pairs=4):
                with dve.Fori(0, pairs) as i:
                    for u in range(2):
                        split_lo(FIRST[stage] + 2 * i + u + 2, u)

            def turning(stage, nat, count, sampled=True):
                with dve.Fori(0, 4) as i:
                    for u in range(2):
                        n = 2 * i + u
                        split_lo(FIRST[stage] + n + 2, u)
                        dve.wait_ge(turned, count + n + 1)
                        nt = QT if sampled else MT
                        last = nc.vector.tensor_copy(nat[:, 0:nt, bass.ds(n * P, P)],
                                                     bank(4 + u)[:, 0:nt * P].rearrange("p (j d) -> p j d", j=nt))
                        if sampled:
                            last = nc.vector.tensor_copy(nat[0:NS, QT, bass.ds(n * P, P)], bank(6 + u)[0:NS, 0:P])
                        last.then_inc(nat_done, 1)

            lows("q")
            lows("k")
            turning("v", v_nat, 0)

            def s_heads(b):
                dve.wait_ge(s_pv, b + 1)
                nc.vector.tensor_tensor(masked_s[:, :].rearrange("p (h d) -> p h d", h=HEADS),
                                        ps4[0:64, 0:2, :].rearrange("p a (h d) -> p (a h) d", d=DV),
                                        cst[0:64, C_M8:C_M8 + 8].unsqueeze(2).to_broadcast([64, HEADS, DV]),
                                        ALU.mult).then_inc(s_masked, 1)
                dve.wait_ge(s_masked, b + 1)
                nc.vector.tensor_reduce(o_s[:, 0, :], masked_s[:, :].rearrange("p (h d) -> p d h", h=HEADS),
                                        AX.X, ALU.add).then_inc(s_osum, 1)

            def s_norm(b):
                dve.wait_ge(s_orms, b + 1)
                wait(dve, s_oT, b)
                nc.vector.tensor_scalar(o_s[:, 1, :], o_s[:, 0, :], col(S_R, 64), None, ALU.mult)\
                    .then_inc(s_onorm, 1)

            def s_combined(b):
                dve.wait_ge(s_comb, b + 1)
                wait(dve, s_pv, b)
                nc.vector.tensor_copy(aT_s[:, 0:PAGES * 64], bank(2)[:, 0:PAGES * 64])
                nc.vector.tensor_copy(aT_s[0:TS, PAGES * 64:], bank(3)[0:TS, 0:64]).then_inc(s_aT, 1)

            def s_body(i):
                for e in range(2):
                    b = 2 * i + e
                    dve.wait_ge(s_scores, b + 1)
                    wait(dve, s_comb, b - 1)
                    settle(dve, b)
                    nc.vector.tensor_tensor_reduce(out=logit_s[:, e, :].rearrange("p (c n) -> p c n", c=2),
                                                   in0=acc[0][:, :, 0:HK],
                                                   in1=bias_s[:, :].rearrange("p (c n) -> p c n", c=2),
                                                   scale=1.0, scalar=NEG, op0=ALU.add, op1=ALU.max,
                                                   accum_out=col(S_MAX)).then_inc(s_logit, 1)
                    dve.wait_ge(s_logit, b + 1)
                    nc.vector.tensor_scalar(col(S_NEG), col(S_MAX), -1.0, None, ALU.mult).then_inc(s_neg, 1)
                    if not isinstance(b, int) or b >= 2:
                        s_heads(b - 2)
                    if not isinstance(b, int) or b >= 1:
                        s_combined(b - 1)
                    dve.wait_ge(s_exp, b + 1)
                    nc.vector.reciprocal(col(S_RC), col(S_SUM)).then_inc(s_rc, 1)
                    dve.wait_ge(s_rc, b + 1)
                    nc.vector.tensor_scalar(coef_s[:, :], cst[:, C_COMB:C_COMB + 64], col(S_RC), col(N_LAMS),
                                            ALU.mult, ALU.mult).then_inc(s_coef, 1)
                    if not isinstance(b, int) or b >= 2:
                        s_norm(b - 2)

            dve.wait_ge(v_zero, 2)
            dve.wait_ge(bias_s_loaded, 16)
            dve.wait_ge(lam_ready, 4)
            peeled(dve, NB // 2, s_body, 2)
            s_heads(NB - 2)
            s_combined(NB - 1)
            s_norm(NB - 2)
            s_heads(NB - 1)
            s_norm(NB - 1)

            def p_body(hp0, last_pair=False):
                def logits(n):
                    hp, n = hp0 + n // 8, n % 8
                    m, e, w = n % 2, n // 4, (n % 4 + 1) * P
                    dve.wait_ge(p_scores, 8 * hp + n + 1)
                    if n % 4 == 0:
                        dve.wait_ge(p_bias[e], 16 * hp + 16)
                    wait(dve, p_a, 8 * hp + n - 1)
                    settle(dve, hp)
                    for c in range(2):
                        last = nc.vector.tensor_tensor_reduce(
                            out=logit_p[:, m, c, 0:w], in0=bank(4 + 2 * m + c)[:, 0:w],
                            in1=bias_p[:, e, SEQ - w:SEQ], scale=1.0, scalar=NEG, op0=ALU.add, op1=ALU.max,
                            accum_out=col(P_MAX + 2 * m + c))
                    last.then_inc(p_logit, 1)
                    dve.wait_ge(p_logit, 8 * hp + n + 1)
                    nc.vector.tensor_scalar(col(P_NEG + 2 * m, w=2), col(P_MAX + 2 * m, w=2), -1.0, None, ALU.mult)\
                        .then_inc(p_neg, 1)

                def combine(n):
                    hp = hp0
                    m, w = n % 2, (n % 4 + 1) * P
                    dve.wait_ge(p_exp, 8 * hp + n + 1)
                    nc.vector.reciprocal(col(P_RC + 2 * m, w=2), col(P_SUM + 2 * m, w=2)).then_inc(p_rc, 1)
                    dve.wait_ge(p_rc, 8 * hp + n + 1)
                    wait(dve, p_turn, 8 * hp + n - 1)
                    nc.vector.tensor_scalar(a_p[:, m, 0:w], logit_p[:, m, 1, 0:w], col(P_RC + 2 * m + 1), col(N_LAM),
                                            ALU.mult, ALU.mult).then_inc(p_a1, 1)
                    dve.wait_ge(p_a1, 8 * hp + n + 1)
                    nc.vector.scalar_tensor_tensor(a_p[:, m, 0:w], logit_p[:, m, 0, 0:w], col(P_RC + 2 * m),
                                                   a_p[:, m, 0:w], ALU.mult, ALU.add).then_inc(p_a, 1)

                def norm(e, hp):
                    dve.wait_ge(p_orms, 2 * hp + e + 1)
                    nc.vector.tensor_tensor(o_p[:, e, :].rearrange("p (i d) -> p i d", i=QT),
                                            bank(e).rearrange("p (i d) -> p i d", i=QT),
                                            col(P_R + 4 * e, w=4).unsqueeze(2).to_broadcast([P, QT, DV]),
                                            ALU.mult).then_inc(p_onorm, 1)

                first_pair = isinstance(hp0, int) and hp0 == 0
                if first_pair:
                    logits(0)
                for n in range(8):
                    if n < 7 or not last_pair:
                        logits(n + 1)
                    combine(n)
                    if n == 2 and not first_pair:
                        norm(1, hp0 - 1)
                    if n == 5:
                        norm(0, hp0)
                if last_pair:
                    norm(1, hp0)

            dve.wait_ge(s_oout, NB)
            pairs(dve, p_body)

            def o_split(src, count):
                for k in range(KT):
                    dve.wait_ge(o_hi_done, count + k + 1)
                    nc.vector.tensor_tensor(o_lo[:, k, :], src[:, k, :], o_hi[:, k, :].bitcast(F32), ALU.subtract)\
                        .then_inc(o_lo_done, 1)

            def branch(stage, first_branch=False):
                with dve.Fori(0, KT) as i:
                    p = FIRST[stage] + 2 * i
                    split_lo(p + 2, 0)
                    split_lo(p + 3, 1)
                    dve.wait_ge(mm_done, p + 2)
                    dve.wait_ge(acc_free[0], FIRST[stage] // 2 + i + 1)
                    into = merged[:, bass.ds(i, 1), :].rearrange("p a n -> p (a n)")
                    if first_branch:
                        nc.vector.tensor_tensor(halves(into), acc_t(1), halves(gate[:, :]), ALU.mult)\
                            .then_inc(acc_free[1], 1)
                    else:
                        dve.wait_ge(w_lo_done, p + 4)
                        nc.vector.tensor_tensor(halves(scaled[:, 0, :]), acc_t(1), halves(gate[:, :]), ALU.mult)\
                            .then_inc(acc_free[1], 1)
                        dve.wait_ge(acc_free[1], FIRST[stage] // 2 + i + 1)
                        nc.vector.tensor_tensor(into, into, scaled[:, 0, :], ALU.add).then_inc(merged_done, 1)

            o_split(qT, 0)
            branch("da_branch", True)

            turning("s", s_nat, KT)
            dve.wait_ge(g_rs, 1)
            dve.wait_ge(sg_loaded, 48)
            for j in range(QT + 1):
                rows = P if j < QT else NS
                last = nc.vector.scalar_tensor_tensor(s_nat[0:rows, j, :], s_nat[0:rows, j, :], col(G_RS + j, rows),
                                                      norm_b[0:rows, :], ALU.mult, ALU.mult)
            last.then_inc(g_norm, 1)

            def gate_mix(n, u):
                dve.wait_ge(g_mix, n + 1)
                dve.wait_ge(acc_free[u], (FIRST["u"] + n) // 2 + 1 if isinstance(n, int)
                            else FIRST["u"] // 2 + (n - u) // 2 + 1)
                wait(dve, g_out, n)
                bias = sgb_b[:, bass.ds(n, 1), :]
                nc.vector.tensor_tensor(mixed[:, 0:SEQ].rearrange("p (j d) -> p j d", j=QT),
                                        bank(4 + u).rearrange("p (j d) -> p j d", j=QT),
                                        bias.to_broadcast([P, QT, P]), ALU.add)
                nc.vector.tensor_tensor(mixed[:, SEQ:T].rearrange("p (b t) -> p b t", b=NB),
                                        bank(6 + u)[:, 0:NS].rearrange("p (b t) -> p b t", b=NB),
                                        bias[:, :, 0:TS].to_broadcast([P, NB, TS]), ALU.add).then_inc(g_bias, 1)
                dve.wait_ge(g_bias, n + 1)
                into = uT[:, bass.ds(n, 1), :].rearrange("p a n -> p (a n)")
                nc.vector.tensor_tensor(into, into, mixed[:, :], ALU.mult).then_inc(g_out, 1)

            def u_body(i):
                for u in range(2):
                    split_lo(FIRST["u"] + 2 * i + u + 2, u)
                    if not isinstance(i, int) or u:
                        gate_mix(2 * i + u - 1, 1 - u)
            peeled(dve, 4, u_body)
            gate_mix(KT - 1, 1)
            o_split(uT, KT)
            branch("sg_branch")

            def zm_body(i):
                for u in range(2):
                    split_lo(FIRST["zm"] + 2 * i + u + 2, u)
            zm_body(0)
            norm_stats(1, MEM)
            zm_body(1)
            norm_scale(m_x, G_MEM, MEM, KT, 2)
            with dve.Fori(2, 4) as i:
                zm_body(i)
            lows("mk")
            turning("mv", vm_nat, 2 * KT, sampled=False)

            def m_out(b, e):
                dve.wait_ge(m_pv, b + 1)
                nc.vector.tensor_tensor(masked_m[:, :].rearrange("p (h d) -> p h d", h=MXH),
                                        acc[0][0:32, :, :].rearrange("p a (h d) -> p (a h) d", d=MXD),
                                        cst[0:32, C_M4:C_M4 + 4].unsqueeze(2).to_broadcast([32, MXH, MXD]),
                                        ALU.mult).then_inc(m_masked, 1)
                dve.wait_ge(m_masked, b + 1)
                wait(dve, m_oT, b - 1)
                nc.vector.tensor_reduce(o_m[:, e, :], masked_m[:, :].rearrange("p (h d) -> p d h", h=MXH),
                                        AX.X, ALU.add).then_inc(m_o, 1)

            def m_body(i):
                for e in range(2):
                    b = 2 * i + e
                    dve.wait_ge(m_scores, b + 1)
                    nc.vector.tensor_reduce(col(M_NEG + e, 32), bank(4 + e)[0:32, 0:MEM], AX.X, ALU.max, negate=True)\
                        .then_inc(m_neg, 1)
                    dve.wait_ge(m_exp, b + 1)
                    nc.vector.reciprocal(col(M_RC + e, 32), col(M_SUM + e, 32)).then_inc(m_rc, 1)
                    dve.wait_ge(m_rc, b + 1)
                    nc.vector.tensor_scalar(p_mb[:, e, :], p_mb[:, e, :], col(M_RC + e, 32), None, ALU.mult)\
                        .then_inc(m_p, 1)
                    if not isinstance(i, int) or e:
                        m_out(b - 1, 1 - e)
            peeled(dve, NB // 2, m_body)
            m_out(NB - 1, 1)

            def c_body(h):
                dve.wait_ge(c_scores, h + 1)
                nc.vector.tensor_reduce(col(MP_NEG, w=QT), ps4[:, 0:2, :].rearrange("p a (i m) -> p (a i) m", m=MEM),
                                        AX.X, ALU.max, negate=True).then_inc(c_neg, 1)
                dve.wait_ge(c_exp, h + 1)
                nc.vector.reciprocal(col(MP_RC, w=QT), col(MP_SUM, w=QT)).then_inc(c_rc, 1)
                dve.wait_ge(c_rc, h + 1)
                nc.vector.tensor_tensor(p_m[:, :, :], p_m[:, :, :],
                                        col(MP_RC, w=QT).unsqueeze(2).to_broadcast([P, QT, MEM]), ALU.mult)\
                    .then_inc(c_p, 1)
            with dve.Fori(0, MXH) as h:
                c_body(h)

            o_split(zmT, 2 * KT)
            branch("mx_branch")

            dve.wait_ge(stored, 80)
            for k in range(KT):
                dve.wait_ge(o_hi_done, 3 * KT + k + 1)
                nc.vector.tensor_tensor(m2_lo[:, k, :], merged[:, k, :], m2_hi[:, k, :].bitcast(F32), ALU.subtract)\
                    .then_inc(o_lo_done, 1)

            with dve.Fori(0, 4) as i:
                for u in range(2):
                    p = FIRST["w_out"] + 2 * i + u
                    split_lo(p + 2, u)
                    dve.wait_ge(mm_done, p + 1)
                    into = halves(x_sb[:, bass.ds(2 * i + u, 1), :].rearrange("p a n -> p (a n)"))
                    nc.vector.tensor_tensor(into, acc_t(u), into, ALU.add).then_inc(acc_free[u], 1)
            norm_stats(2, T)
            norm_scale(x_sb, G_FFN, T, 2 * KT, 3)

            with dve.Fori(0, FT) as i:
                p = FIRST["up"] + 2 * i
                split_lo(p + 2, 0)
                split_lo(p + 3, 1)
                dve.wait_ge(mm_done, p + 2)
                dve.wait_ge(acc_free[0], FIRST["up"] // 2 + i + 1)
                dve.wait_ge(w_lo_done, p + 4)
                nc.vector.tensor_tensor(halves(scaled[:, 0, :]), acc_t(1), halves(gate[:, :]), ALU.mult)\
                    .then_inc(acc_free[1], 1)
                dve.wait_ge(ffn_hi, i + 1)
                nc.vector.tensor_tensor(g_lo[:, bass.ds(i, 1), :].rearrange("p a n -> p (a n)"), scaled[:, 0, :],
                                        g_hi[:, bass.ds(i, 1), :].rearrange("p a n -> p (a n)").bitcast(F32),
                                        ALU.subtract).then_inc(ffn_lo, 1)

            def down_body(i):
                for f in range(2):
                    for c in range(3):
                        q = 3 * f + c
                        p = FIRST["down"] + 6 * i + q
                        if isinstance(i, int) and p + 2 >= PANELS:
                            continue
                        split_lo(p + 2, q % 2)
                    dve.wait_ge(mm_done, FIRST["down"] + 6 * i + 3 * f + 3)
                    into = halves(x_sb[:, bass.ds(2 * i + f, 1), :].rearrange("p a n -> p (a n)"))
                    nc.vector.tensor_tensor(into, acc_t(f), into, ALU.add).then_inc(down_free[f], 1)
            with dve.Fori(0, 3) as i:
                down_body(i)
            down_body(3)
            norm_stats(3, T)
            dve.wait_ge(rms_ready, 4)
            for k in range(KT):
                nc.vector.scalar_tensor_tensor(y_sb[:, k, :], x_sb[:, k, :], par[:, G_FINAL + k:G_FINAL + k + 1],
                                               rms_b[:, :], ALU.mult, ALU.mult).then_inc(y_ready, 1)

        @block.gpsimd
        def _(pool):
            def norm_sum(count, n_cols):
                for k in range(KT):
                    pool.wait_ge(squared, count + k + 1)
                    src = (square if k % 2 == 0 else gate)[:, 0:n_cols]
                    if k == 0:
                        last = nc.gpsimd.tensor_copy(ssum[:, 0:n_cols], src)
                    else:
                        pool.wait_ge(summed, count + k)
                        last = nc.gpsimd.tensor_tensor(ssum[:, 0:n_cols], ssum[:, 0:n_cols], src, ALU.add)
                    last.then_inc(summed, 1)

            def norm_pow(count, n_cols):
                nt = 5 if n_cols == T else 2
                pool.wait_ge(stat_ready, count + 1)
                nc.gpsimd.tensor_tensor(col(N_RS, w=nt), col(N_STAT, w=nt), col(N_HALF, w=nt), ALU.pow)\
                    .then_inc(stat_pow, 1)

            def norm_lo(lo, hi, n_cols, count):
                for k in range(KT):
                    pool.wait_ge(n_hi, count + k + 1)
                    nc.gpsimd.tensor_tensor(lo[:, k, :], scaled[:, k % 2, 0:n_cols], hi[:, k, :].bitcast(F32),
                                            ALU.subtract).then_inc(n_lo, 1)

            nc.gpsimd.memset(small[:, :], 1.0).then_inc(const_set, 1)
            pool.wait_ge(const_set, 1)
            nc.gpsimd.memset(col(N_HALF, w=5), -0.5).then_inc(const_set, 1)
            nc.gpsimd.memset(q_blk[:, :, :], 0.0).then_inc(const_set, 1)
            norm_sum(0, T)
            norm_pow(0, T)
            norm_lo(h_lo, h_hi, T, 0)
            pool.wait_ge(stat_mm, 1)
            nc.gpsimd.memset(v_new[:, :], 0.0).then_inc(v_zero, 1)
            nc.gpsimd.memset(aT_s[:, PAGES * 64:], 0.0).then_inc(v_zero, 1)

            pool.wait_ge(acc_free[0], FIRST["v"] // 2)
            pool.wait_ge(acc_free[1], FIRST["v"] // 2)
            pool.dma_start(kT_out.rearrange("(k p) n -> p k n", p=P), kT[:, :, :]).then_inc(stored, 16)
            def s_queries(b):
                wait(pool, s_scores, b)
                wait(pool, s_q, 3 * b)
                nc.gpsimd.tensor_copy(k_pg[:, :, PAST:KEYS], kT[:, :, bass.ds(SEQ + b * TS, TS)]).then_inc(s_q, 1)
                for c in range(2):
                    rows = slice(c * DK, (c + 1) * DK)
                    if c == 1:
                        pool.wait_ge(s_q, 3 * b + 2)
                    nc.gpsimd.tensor_copy(view(q_blk[rows, 0, :], [[P + 2 * TS, HEADS], [1, TS]], c * TS),
                                          qT[rows, :, bass.ds(SEQ + b * TS, TS)]).then_inc(s_q, 1)

            pool.wait_ge(const_set, 3)
            pool.wait_ge(v_zero, 2)
            s_queries(0)
            pool.wait_ge(nat_done, KT)
            pool.dma_start(vs_out, v_nat[0:NS, QT, :]).then_inc(vs_stored, 16)
            pool.dma_start(v_out.rearrange("(j p) n -> p j n", p=P), v_nat[:, 0:QT, :]).then_inc(stored, 16)

            def s_power(b):
                pool.wait_ge(s_oss, b + 1)
                settle(pool, b)
                nc.gpsimd.tensor_scalar(col(S_ST, 64), col(S_SS, 64), 1.0 / DV, EPS, ALU.mult, ALU.add)\
                    .then_inc(s_ost, 1)
                pool.wait_ge(s_ost, b + 1)
                nc.gpsimd.tensor_tensor(col(S_R, 64), col(S_ST, 64), col(N_HALF, 64), ALU.pow).then_inc(s_orms, 1)

            def s_body(b):
                s_queries(b)
                s_power(b - 3)
            s_queries(1)
            s_queries(2)
            with pool.Fori(3, NB) as b:
                s_body(b)
            for b in range(NB - 3, NB):
                s_power(b)

            pool.wait_ge(s_oout, NB)
            for e in range(2):
                for c in range(2):
                    wait(pool, p_zero, 2 * e + c)
                    nc.gpsimd.memset(q_z[(1 - c) * DK:(2 - c) * DK, e, c, :], 0.0).then_inc(p_zero, 1)

            def p_queries(hp, e):
                wait(pool, p_scores, 4 * (2 * hp + e - 1))
                for c in range(2):
                    rows = slice(c * DK, (c + 1) * DK)
                    wait(pool, p_q, 4 * hp + 2 * e + c)
                    nc.gpsimd.tensor_copy(q_z[rows, e, c, :],
                                          qT[rows, bass.ds(2 * hp + e, 1), 0:SEQ].rearrange("p a n -> p (a n)"))\
                        .then_inc(p_q, 1)

            def p_power(hp, e, last_pair):
                h = 2 * hp + e
                pool.wait_ge(p_q, 2 * HEADS if last_pair else 4 * hp + 2 * e + 6)
                pool.wait_ge(p_oss, h + 1)
                settle(pool, hp)
                nc.gpsimd.tensor_scalar(col(P_ST, w=4), col(P_SS + 4 * e, w=4), 1.0 / DV, EPS, ALU.mult, ALU.add)\
                    .then_inc(p_ost, 1)
                pool.wait_ge(p_ost, h + 1)
                nc.gpsimd.tensor_tensor(col(P_R + 4 * e, w=4), col(P_ST, w=4), col(N_HALF, w=4), ALU.pow)\
                    .then_inc(p_orms, 1)

            def p_body(hp, last_pair=False):
                for e in range(2):
                    if not last_pair:
                        p_queries(hp + 1, e)
                    p_power(hp, e, last_pair)
            pool.wait_ge(p_zero, 4)
            p_queries(0, 0)
            p_queries(0, 1)
            pairs(pool, p_body)

            pool.wait_ge(o_lo_done, KT)
            nc.gpsimd.memset(sg_ws[:, :, :], 0.0).then_inc(g_zero, 1)
            pool.wait_ge(sg_loaded, 48)
            nc.gpsimd.affine_select(out=sg_w[:, :, :], in_=sg_w[:, :, :], compare_op=ALU.is_ge, fill=0.0, base=0,
                                    pattern=[[0, GROUPS], [1, P]], channel_multiplier=-1).then_inc(g_wmask, 1)
            pool.wait_ge(sgs_loaded, 16 * NB)
            nc.gpsimd.affine_select(out=sg_ws[:, :, :], in_=sg_ws[:, :, :], compare_op=ALU.is_ge, fill=0.0, base=0,
                                    pattern=[[0, GROUPS], [1, NS]], channel_multiplier=-1).then_inc(g_wmask, 1)
            pool.wait_ge(g_ss, 1)
            nc.gpsimd.tensor_scalar(col(G_ST, w=5), col(G_SS, w=5), 1.0 / D, EPS, ALU.mult, ALU.add)\
                .then_inc(g_st, 1)
            pool.wait_ge(g_st, 1)
            nc.gpsimd.tensor_tensor(col(G_RS, w=5), col(G_ST, w=5), col(N_HALF, w=5), ALU.pow).then_inc(g_rs, 1)
            pool.wait_ge(g_norm, 1)
            pool.dma_start(vn_out, s_nat[0:NS, QT, :]).then_inc(stored, 16)

            def slots(i):
                for u in range(2):
                    n = 2 * i + u
                    wait(pool, g_mix, n - 1)
                    nc.gpsimd.tensor_copy(s_slot[:, u, 0:QT, :], s_nat[:, 0:QT, bass.ds(n * P, P)])\
                        .then_inc(g_slot, 1)
                    nc.gpsimd.tensor_copy(s_slot[0:NS, u, QT, :], s_nat[0:NS, QT, bass.ds(n * P, P)])\
                        .then_inc(g_slot, 1)
            peeled(pool, 4, slots)

            norm_sum(KT, MEM)
            norm_pow(1, MEM)
            norm_lo(m_lo, m_hi, MEM, KT)
            for u in range(2):
                pool.wait_ge(acc_free[u], FIRST["mv"] // 2)
            pool.wait_ge(mm_done, FIRST["mv"])
            pool.dma_start(mkT_out.rearrange("(k p) n -> p k n", p=P), kmT[:, :, :]).then_inc(stored, 16)
            pool.wait_ge(nat_done, 3 * KT)
            pool.wait_ge(mm_done, FIRST["mx_branch"])
            pool.dma_start(mv_out.rearrange("(m p) n -> p m n", p=P), vm_nat[:, :, :]).then_inc(stored, 16)
            nc.gpsimd.memset(q_mb[:, :, :, :], 0.0).then_inc(m_zero, 1)
            pool.wait_ge(m_zero, 1)

            def m_body(i):
                for e in range(2):
                    b = 2 * i + e
                    wait(pool, m_scores, b - 1)
                    nc.gpsimd.tensor_copy(view(q_mb[:, e, 0, :], [[2 * 32 + TS, MXH], [32, 2], [1, TS]]),
                                          zmT[:, :, bass.ds(SEQ + b * TS, TS)].rearrange("p (h f) t -> p h f t", f=2))\
                        .then_inc(m_q, 1)
            peeled(pool, NB // 2, m_body)

            def c_body(h):
                wait(pool, c_scores, h)
                nc.gpsimd.tensor_copy(q_m[:, :, :], zmT[:, bass.ds(2 * h, 2), 0:SEQ]).then_inc(c_q, 1)
                wait(pool, c_pv, h)
                nc.gpsimd.tensor_copy(v_m[:, :, :], vm_nat[:, :, bass.ds(h * MXD, MXD)]).then_inc(c_v, 1)
            peeled(pool, MXH, c_body)

            def resid_sum(n, count):
                pool.wait_ge(squared, count + n + 1)
                wait(pool, summed, count + n)
                nc.gpsimd.tensor_tensor(ssum[:, :], ssum[:, :], square[:, :], ALU.add).then_inc(summed, 1)

            pool.wait_ge(stat_mm, 2)
            nc.gpsimd.memset(ssum[:, :], 0.0).then_inc(m_zero, 1)
            pool.wait_ge(m_zero, 2)
            with pool.Fori(0, KT) as n:
                resid_sum(n, 2 * KT)
            norm_pow(2, T)
            norm_lo(h_lo, h_hi, T, 2 * KT)
            pool.wait_ge(stat_mm, 3)
            nc.gpsimd.memset(ssum[:, :], 0.0).then_inc(m_zero, 1)
            pool.wait_ge(m_zero, 3)
            with pool.Fori(0, KT) as n:
                resid_sum(n, 3 * KT)
            norm_pow(3, T)

        @block.tensor
        def _(pe):
            def panel(p, u, x_hi, x_lo, a=None, nk=KT, k0=0, n=HT, nc_=2, start=True, stop=True):
                a = u if a is None else a
                pe.wait_ge(w_lo_done, p + 1)
                for k in range(nk):
                    for t, (w, x) in enumerate(((w_hi, x_hi), (w_hi, x_lo), (w_lo, x_hi))):
                        for c in range(nc_):
                            last = nc.tensor.matmul(acc[a][:, c, 0:n], w[:, u, k * P:(k + 1) * P],
                                                    x[:, k0 + k, c * n:(c + 1) * n],
                                                    start=start and k == 0 and t == 0,
                                                    stop=stop and k == nk - 1 and t == 2)
                last.then_inc(mm_done, 1)

            def slot_free(stage, i, u):
                wait(pe, acc_free[u], FIRST[stage] // 2 + i)

            def plain(stage, x_hi, x_lo, first=0, last=4, **kw):
                def body(i):
                    for u in range(2):
                        slot_free(stage, i, u)
                        panel(FIRST[stage] + 2 * i + u, u, x_hi, x_lo, **kw)
                if FIRST[stage] == 0:
                    peeled(pe, last, body)
                else:
                    with pe.Fori(first, last) as i:
                        body(i)

            def turn_tile(stage, n, u, count, nt):
                k = (FIRST[stage] + n) // 2 if isinstance(n, int) else FIRST[stage] // 2 + (n - u) // 2
                pe.wait_ge(acc_free[u], k + 1)
                wait(pe, nat_done, count + n - 1)
                for j in range(min(nt, QT)):
                    last = nc.tensor.transpose(bank(4 + u)[:, j * P:(j + 1) * P], turn[:, u, j * P:(j + 1) * P], ident)
                if nt > QT:
                    last = nc.tensor.transpose(bank(6 + u)[0:NS, 0:P], turn[:, u, SEQ:T], ident)
                last.then_inc(turned, 1)

            def turning(stage, x_hi, x_lo, count, nt=QT + 1, **kw):
                def body(i):
                    for u in range(2):
                        slot_free(stage, i, u)
                        panel(FIRST[stage] + 2 * i + u, u, x_hi, x_lo, **kw)
                        if not isinstance(i, int) or u:
                            turn_tile(stage, 2 * i + u - 1, 1 - u, count, nt)
                peeled(pe, 4, body)
                turn_tile(stage, KT - 1, 1, count, nt)

            def norm_stats(count, n_cols):
                pe.wait_ge(summed, (count + 1) * KT)
                starts = (0, P, 2 * P, 3 * P, T - P) if n_cols == T else (0, P)
                for j, t0 in enumerate(starts):
                    last = nc.tensor.matmul(bank(4)[:, j:j + 1], ssum[:, t0:t0 + P], cst[:, C_INVD:C_INVD + 1],
                                            start=True, stop=True)
                last.then_inc(stat_mm, 1)

            def norm_bcast(count, n_cols):
                pe.wait_ge(diag_ready, count + 1)
                ones = cst[:, C_ONE:C_ONE + P]
                flat = diag[:, :, :].rearrange("p j n -> p (j n)")
                if n_cols == T:
                    nc.tensor.matmul(bank(5), ones, flat[:, 0:SEQ], start=True, stop=True)
                    last = nc.tensor.matmul(bank(6)[:, 0:NS], ones, flat[:, QT * P + P - NS:QT * P + P],
                                            start=True, stop=True)
                else:
                    last = nc.tensor.matmul(bank(5)[:, 0:MEM], ones, flat[:, 0:MEM], start=True, stop=True)
                last.then_inc(bcast_mm, 1)

            pe.wait_ge(cst_loaded, 64)
            pe.wait_ge(lam_neg, 1)
            nc.tensor.matmul(bank(2)[:, 0:1], cst[0:1, C_ONE:C_ONE + P], lam_w[0:1, 2 * DK + 5:2 * DK + 6],
                             start=True, stop=True).then_inc(lam_mm, 1)
            for half, b in enumerate((7, 3)):
                last = nc.tensor.matmul(bank(b)[0:HEADS, 0:HREV], par[0:BUCKETS + 1, G_REL:G_REL + HEADS],
                                        b_sel[:, half * HREV:(half + 1) * HREV], start=True, stop=True)
            last.then_inc(line_mm, 1)
            norm_stats(0, T)
            norm_bcast(0, T)
            pe.wait_ge(n_lo, KT)
            pe.wait_ge(lam_ready, 1)
            pe.wait_ge(line_ready, 2)
            plain("q", h_hi, h_lo)
            plain("k", h_hi, h_lo)
            turning("v", h_hi, h_lo, 0)

            all_evacuated(pe, "da_branch")
            pe.wait_ge(nat_done, KT)
            pe.wait_ge(v_zero, 2)

            def s_score(b):
                pe.wait_ge(k_loaded, 16 * PAGES * (b + 1))
                pe.wait_ge(s_q, 3 * (b + 1))
                wait(pe, s_logit, b)
                for h in range(HEADS):
                    for c in range(2):
                        last = nc.tensor.matmul(acc[0][:, c, 0:HK], q_blk[:, h, :], k_pg[:, h, c * HK:(c + 1) * HK],
                                                start=h == 0, stop=h == HEADS - 1)
                last.then_inc(s_scores, 1)

            def s_combine(b, e):
                pe.wait_ge(s_coef, b + 1)
                wait(pe, s_aT, b)
                for j in range(PAGES):
                    nc.tensor.matmul(bank(2)[:, j * 64:(j + 1) * 64], logit_s[:, e, j * P:(j + 1) * P], coef_s[:, :],
                                     start=True, stop=True)
                nc.tensor.matmul(bank(3)[0:TS, 0:64], logit_s[:, e, PAST:KEYS], coef_s[:, :], start=True, stop=True)\
                    .then_inc(s_comb, 1)

            def s_values(b):
                pe.wait_ge(s_aT, b + 1)
                pe.wait_ge(v_loaded, 16 * (PAGES + 1) * (b + 1))
                wait(pe, s_masked, b)
                for half in range(2):
                    cols = slice(half * 512, (half + 1) * 512)
                    for j in range(PAGES + 1):
                        v = v_pg[:, j, cols] if j < PAGES else v_new[:, cols]
                        last = nc.tensor.matmul(bank(4 + half)[0:64, :], aT_s[:, j * 64:(j + 1) * 64], v,
                                                start=j == 0, stop=j == PAGES)
                last.then_inc(s_pv, 1)

            def s_turn(b):
                pe.wait_ge(s_onorm, b + 1)
                wait(pe, s_oout, b)
                settle(pe, b)
                nc.tensor.transpose(bank(6)[:, 0:64], o_s[:, 1, :], cst[0:64, C_ID:C_ID + 64]).then_inc(s_oT, 1)

            def s_body(i):
                for e in range(2):
                    b = 2 * i + e
                    s_score(b)
                    if not isinstance(b, int) or b >= 3:
                        s_turn(b - 3)
                    if not isinstance(b, int) or b >= 2:
                        s_values(b - 2)
                    if not isinstance(b, int) or b >= 1:
                        s_combine(b - 1, 1 - e)
            peeled(pe, NB // 2, s_body, 2)
            s_turn(NB - 3)
            s_values(NB - 2)
            s_combine(NB - 1, 1)
            s_turn(NB - 2)
            s_values(NB - 1)
            s_turn(NB - 1)

            pe.wait_ge(s_oout, NB)
            pe.wait_ge(p_zero, 4)

            def p_body(hp0, last_pair=False):
                def score(n):
                    hp, n = hp0 + n // 8, n % 8
                    m, e, i = n % 2, n // 4, n % 4
                    w = (i + 1) * P
                    pe.wait_ge(p_q, 2 * (2 * hp + e + 1))
                    wait(pe, p_logit, 8 * hp + n - 1)
                    for c in range(2):
                        last = nc.tensor.matmul(bank(4 + 2 * m + c)[:, 0:w], q_z[:, e, c, i * P:(i + 1) * P],
                                                kT[:, bass.ds(2 * hp + e, 1), 0:w].rearrange("p a n -> p (a n)"),
                                                start=True, stop=True)
                    last.then_inc(p_scores, 1)

                def turn_probs(n):
                    hp = hp0
                    m, i = n % 2, n % 4
                    pe.wait_ge(p_a, 8 * hp + n + 1)
                    wait(pe, p_aT, 8 * hp + n - 1)
                    for j in range(i + 1):
                        last = nc.tensor.transpose(bank(2 + m)[:, j * P:(j + 1) * P], a_p[:, m, j * P:(j + 1) * P], ident)
                    last.then_inc(p_turn, 1)

                def values(n):
                    hp, n = hp0 + n // 8, n % 8
                    m, e, i = n % 2, n // 4, n % 4
                    pe.wait_ge(p_aT, 8 * hp + n + 1)
                    if i == 0:
                        wait(pe, p_oout, 2 * hp + e - 1)
                    for j in range(i + 1):
                        last = nc.tensor.matmul(bank(e)[:, i * DV:(i + 1) * DV], aT_p[:, m, j * P:(j + 1) * P],
                                                v_nat[:, j, bass.ds((2 * hp + e) * DV, DV)],
                                                start=j == 0, stop=j == i)
                    last.then_inc(p_pv, 1)

                def turn_out(e, hp):
                    pe.wait_ge(p_onorm, 2 * hp + e + 1)
                    for i in range(QT):
                        last = nc.tensor.transpose(bank(e)[:, i * P:(i + 1) * P], o_p[:, e, i * DV:(i + 1) * DV], ident)
                    last.then_inc(p_oT, 1)

                first_pair = isinstance(hp0, int) and hp0 == 0
                if first_pair:
                    score(0)
                    score(1)
                for n in range(8):
                    if n < 6 or not last_pair:
                        score(n + 2)
                    turn_probs(n)
                    if n > 0 or not first_pair:
                        values(n - 1)
                    if n == 3 and not first_pair:
                        turn_out(1, hp0 - 1)
                    if n == 6:
                        turn_out(0, hp0)
                if last_pair:
                    values(7)
                    turn_out(1, hp0)
            pairs(pe, p_body)

            def branch(stage, split):
                def body(i):
                    slot_free(stage, i, 0)
                    panel(FIRST[stage] + 2 * i, 0, h_hi, h_lo)
                    slot_free(stage, i, 1)
                    pe.wait_ge(o_lo_done, split)
                    panel(FIRST[stage] + 2 * i + 1, 1, o_hi, o_lo)
                with pe.Fori(0, KT) as i:
                    body(i)

            pe.wait_ge(p_oout, HEADS)
            branch("da_branch", KT)

            turning("s", h_hi, h_lo, KT)
            pe.wait_ge(nat_done, 2 * KT)
            pe.wait_ge(g_wmask, 2)

            def mix(n, u):
                pe.wait_ge(g_slot, 2 * (n + 1))
                wait(pe, g_bias, n - 1)
                group = bass.ds(n, 1)
                for j in range(QT):
                    nc.tensor.matmul(bank(4 + u)[:, j * P:(j + 1) * P], s_slot[:, u, j, :],
                                     sg_w[:, group, :].rearrange("p a n -> p (a n)"), start=True, stop=True)
                nc.tensor.matmul(bank(6 + u)[:, 0:NS], s_slot[0:NS, u, QT, :],
                                 sg_ws[:, group, :].rearrange("p a n -> p (a n)"), start=True, stop=True)\
                    .then_inc(g_mix, 1)

            def u_body(i):
                for u in range(2):
                    slot_free("u", i, u)
                    panel(FIRST["u"] + 2 * i + u, u, h_hi, h_lo)
                    if not isinstance(i, int) or u:
                        mix(2 * i + u - 1, 1 - u)
            peeled(pe, 4, u_body)
            mix(KT - 1, 1)
            branch("sg_branch", 2 * KT)

            plain("zm", h_hi, h_lo, 0, 1)
            norm_stats(1, MEM)
            plain("zm", h_hi, h_lo, 1, 2)
            norm_bcast(1, MEM)
            plain("zm", h_hi, h_lo, 2, 4)
            pe.wait_ge(n_lo, 2 * KT)
            plain("mk", m_hi, m_lo, n=MEM, nc_=1)
            turning("mv", m_hi, m_lo, 2 * KT, MT, n=MEM, nc_=1)
            all_evacuated(pe, "mx_branch")
            pe.wait_ge(nat_done, 3 * KT)

            def m_score(b, e, i):
                pe.wait_ge(km_loaded[e], 16 * i + 16)
                pe.wait_ge(m_q, b + 1)
                wait(pe, m_exp, b - 1)
                for f in range(KT):
                    last = nc.tensor.matmul(bank(4 + e)[0:32, 0:MEM], q_mb[:, e, f, :], km_pg[:, e, f, :],
                                            start=f == 0, stop=f == KT - 1)
                last.then_inc(m_scores, 1)

            def m_turn_p(b, e):
                pe.wait_ge(m_p, b + 1)
                wait(pe, m_pT, b)
                settle(pe, b)
                for m in range(MT):
                    last = nc.tensor.transpose(bank(6)[:, m * 32:(m + 1) * 32], p_mb[:, e, m * P:(m + 1) * P],
                                               cst[0:32, C_ID:C_ID + 32])
                last.then_inc(m_turn, 1)

            def m_values(b, e, i):
                pe.wait_ge(m_pT, b + 1)
                pe.wait_ge(vm_loaded[e], 16 * i + 16)
                wait(pe, m_masked, b)
                for half in range(2):
                    for m in range(MT):
                        last = nc.tensor.matmul(bank(half)[0:32, :], pT_mb[:, e, m * 32:(m + 1) * 32],
                                                vm_pg[:, e, m, half * 512:(half + 1) * 512], start=m == 0, stop=m == 1)
                last.then_inc(m_pv, 1)

            def m_turn_o(b, e):
                pe.wait_ge(m_o, b + 1)
                wait(pe, m_oout, b)
                settle(pe, b)
                for f in range(2):
                    last = nc.tensor.transpose(bank(7)[:, f * 32:(f + 1) * 32], o_m[:, e, f * P:(f + 1) * P],
                                               cst[0:32, C_ID:C_ID + 32])
                last.then_inc(m_oT, 1)

            def m_body(i):
                for e in range(2):
                    b = 2 * i + e
                    m_score(b, e, i)
                    if not isinstance(i, int):
                        m_turn_o(b - 2, e)
                    if not isinstance(i, int) or e:
                        m_values(b - 1, 1 - e, i if e else i - 1)
                    m_turn_p(b, e)
            peeled(pe, NB // 2, m_body)
            m_turn_o(NB - 2, 0)
            m_values(NB - 1, 1, NB // 2 - 1)
            m_turn_o(NB - 1, 1)

            pe.wait_ge(m_oout, NB)

            def c_score(h):
                pe.wait_ge(c_q, h + 1)
                wait(pe, c_exp, h)
                for i in range(QT):
                    for f in range(2):
                        last = nc.tensor.matmul(bank(4 + i // 2)[:, (i % 2) * MEM:(i % 2 + 1) * MEM],
                                                q_m[:, f, i * P:(i + 1) * P],
                                                kmT[:, bass.ds(2 * h + f, 1), :].rearrange("p a n -> p (a n)"),
                                                start=f == 0, stop=f == 1)
                last.then_inc(c_scores, 1)

            def c_turn_p(h):
                pe.wait_ge(c_p, h + 1)
                wait(pe, c_pT, h)
                for m in range(MT):
                    for i in range(QT):
                        last = nc.tensor.transpose(bank(6 + m)[:, i * P:(i + 1) * P], p_m[:, i, m * P:(m + 1) * P], ident)
                last.then_inc(c_turn, 1)

            def c_values(h):
                pe.wait_ge(c_pT, h + 1)
                pe.wait_ge(c_v, h + 1)
                wait(pe, c_oout, h)
                for f in range(2):
                    for m in range(MT):
                        last = nc.tensor.matmul(bank(f), v_m[:, m, f * P:(f + 1) * P], pT_m[:, m, :],
                                                start=m == 0, stop=m == 1)
                last.then_inc(c_pv, 1)

            def c_body(h):
                c_score(h)
                if not isinstance(h, int):
                    c_values(h - 1)
                c_turn_p(h)
            peeled(pe, MXH, c_body)
            c_values(MXH - 1)
            pe.wait_ge(c_oout, MXH)
            branch("mx_branch", 3 * KT)

            pe.wait_ge(o_lo_done, 4 * KT)
            plain("w_out", m2_hi, m2_lo)
            norm_stats(2, T)
            norm_bcast(2, T)
            pe.wait_ge(n_lo, 3 * KT)
            with pe.Fori(0, FT) as i:
                for u in range(2):
                    slot_free("up", i, u)
                    panel(FIRST["up"] + 2 * i + u, u, h_hi, h_lo)
            all_evacuated(pe, "down")
            pe.wait_ge(ffn_lo, FT)

            def down_body(i):
                for f in range(2):
                    wait(pe, down_free[f], i)
                    k0 = 0
                    for c, nk in enumerate(DOWN_K):
                        q = 3 * f + c
                        panel(FIRST["down"] + 6 * i + q, q % 2, g_hi, g_lo, a=f, nk=nk, k0=k0,
                              start=c == 0, stop=c == 2)
                        k0 += nk
            peeled(pe, 4, down_body)
            norm_stats(3, T)
            norm_bcast(3, T)


def bucket_selection():
    import math
    import numpy as np
    out = np.zeros((BUCKETS + 1, REV), np.float32)
    exact = BUCKETS // 2
    for y in range(REV):
        d = KEYS - 1 - y
        n = max(d, 0)
        if n < exact:
            b = n
        else:
            ratio = np.log(np.float32(n) / np.float32(exact)) / np.float32(math.log(128 / exact))
            b = min(exact + int(np.float32(ratio) * np.float32(BUCKETS - exact)), BUCKETS - 1)
        out[b, y] = 1.0
        if d < 0:
            out[BUCKETS, y] = NEG
    return out


def constants():
    import numpy as np
    c = np.zeros((P, C_END), np.float32)
    c[:, C_ID:C_ID + P] = np.eye(P)
    c[:, C_ONE:C_ONE + P] = 1.0
    for h in range(HEADS):
        for m in range(2):
            for t in range(TS):
                c[h * 16 + m * 8 + t, C_COMB + h * 8 + t] = 1.0
                c[h * 16 + m * 8 + t, C_C1] = float(m)
        c[h * 8:(h + 1) * 8, C_M8 + h] = 1.0
    for h in range(MXH):
        c[h * 8:(h + 1) * 8, C_M4 + h] = 1.0
    c[:, C_INVD] = 1.0 / D
    return c


def weight_stream(w_in, w_mem_kv, w_branch, w_out, w_up, w_down):
    import numpy as np

    def panels(w, start=0, n=KT):
        part = w[:, start:start + n * P]
        return part.reshape(KT, P, n, P).transpose(2, 1, 0, 3).reshape(n, P, D)

    def paired(a, b):
        return np.stack([a, b], 1).reshape(2 * a.shape[0], P, D)

    gates = 6 * D
    branches = [paired(panels(w_in, gates + r * D), panels(w_branch[r * D:(r + 1) * D])) for r in range(3)]
    down = w_down.reshape(FT, P, KT, P).transpose(2, 1, 0, 3)
    down = np.concatenate([down, np.zeros((KT, P, 3 * KT - FT, P), w_down.dtype)], 2)
    down = down.reshape(KT, P, 3, D).transpose(0, 2, 1, 3).reshape(3 * KT, P, D)
    return np.ascontiguousarray(np.concatenate([
        panels(w_in, 0, 24), branches[0], panels(w_in, 4 * D), panels(w_in, 3 * D), branches[1],
        panels(w_in, 5 * D), panels(w_mem_kv, 0, 16), branches[2], panels(w_out),
        paired(panels(w_up, 0, FT), panels(w_up, DFF, FT)), down]))


def kernel(x_prompt, x_sample, mem_prompt, cache_da_k, cache_da_v, cache_mem_k, cache_mem_v, page_table,
           g_attn, w_in, da_lam, da_subln, rel_bias, sg_norm, sg_w, sg_b, g_mem, w_mem_kv, w_branch, w_out,
           g_ffn, w_up, w_down, g_final):
    import numpy as np
    import concourse.bacc as bacc
    from concourse.bass_utils import run_bass_kernel_spmd

    def host(a):
        return np.asarray(a)

    params = np.zeros((P, G_END), np.float32)
    for at, g in ((G_ATTN, g_attn), (G_MEM, g_mem), (G_FFN, g_ffn), (G_FINAL, g_final)):
        params[:, at:at + KT] = host(g).reshape(KT, P).T
    params[:, G_SUB] = host(da_subln)[0]
    params[0:BUCKETS, G_REL:G_REL + HEADS] = host(rel_bias)
    params[BUCKETS, G_REL:G_REL + HEADS] = 1.0
    params[0, G_LAM:G_END] = host(da_lam).reshape(-1)

    n_pool = cache_da_k.shape[1]
    arrays = {
        "xT": np.concatenate([host(x_prompt)[0], host(x_sample).reshape(NS, D)]).T,
        "memT": host(mem_prompt)[0].T,
        "w_stream": weight_stream(host(w_in)[0], host(w_mem_kv)[0], host(w_branch)[0], host(w_out)[0],
                                  host(w_up)[0], host(w_down)[0]),
        "page_table": host(page_table).reshape(1, -1),
        "cache_k": host(cache_da_k)[0].transpose(0, 3, 2, 1).reshape(n_pool, P, HEADS * PAGE),
        "cache_v": host(cache_da_v)[0].reshape(n_pool, PAGE, D),
        "mem_k": host(cache_mem_k)[0].reshape(NB, MEM, KT, P).transpose(0, 3, 2, 1).reshape(NB, P, KT * MEM),
        "mem_v": host(cache_mem_v)[0].reshape(NB, MEM, D),
        "consts": constants(),
        "bias_select": bucket_selection(),
        "params": params,
        "sg_norm": host(sg_norm),
        "sg_bias": host(sg_b)[0],
        "sg_wT": host(sg_w)[0].transpose(2, 0, 1),
    }
    arrays = {k: np.ascontiguousarray(a) for k, a in arrays.items()}
    outputs = {"yT": (D, T), "kT_out": (D, T), "v_out": (SEQ, D), "vs_out": (NS, D), "mkT_out": (D, MEM),
               "mv_out": (MEM, D), "vn_out": (NS, D)}

    nc = bacc.Bacc("TRN2", target_bir_lowering=False, num_devices=1)
    args = [nc.dram_tensor(k, a.shape, mybir.dt.from_np(a.dtype), kind="ExternalInput").ap()
            for k, a in arrays.items()]
    args += [nc.dram_tensor(k, shape, F32, kind="ExternalOutput").ap() for k, shape in outputs.items()]
    decoder_layer(nc, *args)
    got = run_bass_kernel_spmd(nc, [arrays], core_ids=[0]).results[0]

    y, k = got["yT"].T, got["kT_out"].T
    return (y[0:SEQ].reshape(1, SEQ, D), y[SEQ:T].reshape(NB, TS, D),
            k[0:SEQ].reshape(1, 1, SEQ, HEADS, 2 * DK), got["v_out"].reshape(1, 1, SEQ, HEADS, DV),
            k[SEQ:T].reshape(1, NB, TS, HEADS, 2 * DK), got["vs_out"].reshape(1, NB, TS, HEADS, DV),
            got["mkT_out"].T.reshape(1, 1, MEM, MXH, MXD), got["mv_out"].reshape(1, 1, MEM, MXH, MXD),
            got["vn_out"].reshape(1, NB, TS, D))
```

```python
from contextlib import ExitStack

import concourse.bass as bass
from concourse import mybir

F32 = mybir.dt.float32
F32R = mybir.dt.float32r
I32 = mybir.dt.int32
ALU = mybir.AluOpType
ACT = mybir.ActivationFunctionType
AX = mybir.AxisListType

P = 128
D = 1024
KT = D // P
SEQ = 512
NB, TS = 8, 8
NS = NB * TS
T = SEQ + NS
HT = T // 2
QT = SEQ // P
TILE_ORDER = (0, 2, 1, 3)
PAST, PAGE = 512, 128
PAGES = PAST // PAGE
KEYS = PAST + TS
HK = KEYS // 2
HEADS, DK, DV = 8, 64, 128
MEM, MXH, MXD = 256, 4, 256
MT = MEM // P
GROUPS = 8
DFF = 2816
FT = DFF // P
DOWN_K = (8, 8, 6)
EPS = 1e-6
LAM_INIT = 0.2
NEG = -1e30
BUCKETS = 32
REV = KEYS + P
HREV = REV // 2

STAGES = (("q", 8), ("k", 8), ("v", 8), ("da_branch", 16), ("s", 8), ("u", 8), ("sg_branch", 16),
          ("zm", 8), ("mk", 8), ("mv", 8), ("mx_branch", 16), ("w_out", 8), ("up", 2 * FT), ("down", 24))
FIRST = {}
PANELS = 0
for _name, _n in STAGES:
    FIRST[_name] = PANELS
    PANELS += _n

C_ID, C_ONE, C_COMB, C_M8, C_M4, C_C1, C_INVD, C_END = 0, 128, 256, 320, 328, 332, 333, 334
G_ATTN, G_MEM, G_FFN, G_FINAL, G_SUB, G_REL, G_LAM, G_END = 0, 8, 16, 24, 32, 33, 41, 297


def decoder_layer(nc, xT, memT, w_stream, page_table, cache_k, cache_v, mem_k, mem_v, consts,
                  bias_select, params, sg_norm, sg_bias, sg_wT,
                  yT, kT_out, v_out, vs_out, mkT_out, mv_out, vn_out):
    ctx = ExitStack()
    with ctx:
        base = (nc.sbuf_base + 63) // 64 * 64
        top = nc.sbuf_usable_end

        class Region:
            def __init__(self, at):
                self.at = at

            def take(self, name, shape, dtype=F32):
                size = 4
                for n in shape[1:]:
                    size *= n
                t = nc.alloc_sbuf_tensor_at(name, shape, dtype, offset=self.at)
                self.at += (size + 31) // 32 * 32
                assert self.at <= top, (name, self.at, top)
                return t

        whole = Region(base)
        w_raw = whole.take("w_raw", [P, 2, D])
        w_hi = whole.take("w_hi", [P, 2, D], F32R)
        w_lo = whole.take("w_lo", [P, 2, D], F32R)
        cst = whole.take("cst", [P, C_END])
        par = whole.take("par", [P, G_END])
        small = whole.take("small", [P, 104])
        pages = whole.take("pages", [1, NB * PAGES], I32)
        lam_w = whole.take("lam_w", [1, 2 * DK + 8])
        diag_at = whole.at
        diag = whole.take("diag", [P, 5, P])
        x_at = whole.at
        x_sb = whole.take("x_sb", [P, KT, T])
        h_at = whole.at
        h_hi = whole.take("h_hi", [P, KT, T], F32R)
        h_lo = whole.take("h_lo", [P, KT, T], F32R)
        o_at = whole.at
        o_hi = whole.take("o_hi", [P, KT, T], F32R)
        o_lo = whole.take("o_lo", [P, KT, T], F32R)
        merged_at = whole.at
        merged = whole.take("merged", [P, KT, T])
        z_at = whole.at

        tail = Region(top - 4 * 6 * T - 64)
        tail.at = tail.at // 32 * 32
        tail_at = tail.at
        ssum = tail.take("ssum", [P, T])
        square = tail.take("square", [P, T])
        rms_b = tail.take("rms_b", [P, T])
        scaled = tail.take("scaled", [P, 2, T])
        gate = tail.take("gate", [P, T])

        da = Region(merged_at)
        bias_s = da.take("bias_s", [P, KEYS])
        logit_s = da.take("logit_s", [P, 2, KEYS])
        q_blk = da.take("q_blk", [P, HEADS, P])
        coef_s = da.take("coef_s", [P, 64])
        aT_s = da.take("aT_s", [P, (PAGES + 1) * 64])
        b_sel = Region(da.at).take("b_sel", [BUCKETS + 1, REV])
        masked_s = da.take("masked_s", [64, D])
        o_s = da.take("o_s", [64, 2, DV])
        assert da.at <= z_at
        da = Region(z_at)
        qT = da.take("qT", [P, KT, T])
        kT = da.take("kT", [P, KT, T])
        v_nat = da.take("v_nat", [P, QT + 1, D])
        assert da.at <= tail_at, (da.at, tail_at)
        v_new = Region(tail_at).take("v_new", [P, D])
        turn = scaled
        da = Region(o_at)
        k_pg = da.take("k_pg", [P, HEADS, KEYS])
        v_pg = da.take("v_pg", [P, PAGES, D])
        rel_line = da.take("rel_line", [HEADS, REV])
        k_odd = Region(x_at).take("k_odd", [P, HEADS, KEYS])
        assert x_at + 4 * HEADS * KEYS <= h_at
        k_slot = (k_pg, k_odd)
        v_late = Region(o_at).take("v_late", [P, PAGES, D])
        da = Region(o_at)
        bias_p = da.take("bias_p", [P, 2, SEQ])
        q_z = da.take("q_z", [P, 2, 2, SEQ])
        logit_p = da.take("logit_p", [P, 2, 2, SEQ])
        a_p = da.take("a_p", [P, 2, SEQ])
        aT_p = da.take("aT_p", [P, 2, SEQ])
        o_p = da.take("o_p", [P, 2, SEQ])
        assert da.at <= merged_at

        sg = Region(z_at)
        s_nat = sg.take("s_nat", [P, QT + 1, D])
        s_slot = sg.take("s_slot", [P, 2, QT + 1, P])
        uT = sg.take("uT", [P, KT, T])
        norm_b = sg.take("norm_b", [P, D])
        sgb_b = sg.take("sgb_b", [P, GROUPS, P])
        sg_w = sg.take("sg_w", [P, GROUPS, P])
        sg_ws = Region(diag_at).take("sg_ws", [NS, GROUPS, NS])
        mixed = scaled[:, 0, :]
        nat_square = Region(o_at).take("nat_square", [P, QT + 1, D])
        assert sg.at <= tail_at, (sg.at, tail_at)

        mx = Region(z_at)
        zmT = mx.take("zmT", [P, KT, T])
        kmT = mx.take("kmT", [P, KT, MEM])
        m_x = Region(mx.at).take("m_x", [P, KT, MEM])
        vm_nat = mx.take("vm_nat", [P, MT, D])
        mx2 = Region(mx.at)
        m_hi = mx.take("m_hi", [P, KT, MEM], F32R)
        m_lo = mx.take("m_lo", [P, KT, MEM], F32R)
        assert mx.at <= tail_at, (mx.at, tail_at)
        p_mb = mx2.take("p_mb", [32, 2, MEM])
        pT_mb = mx2.take("pT_mb", [P, 2, MT * 32])
        masked_m = mx2.take("masked_m", [32, D])
        o_m = mx2.take("o_m", [32, 2, MXD])
        pT_m = mx2.take("pT_m", [P, MT, SEQ])
        assert mx2.at <= tail_at
        mx2 = Region(o_at)
        km_pg = mx2.take("km_pg", [P, 2, KT, MEM])
        vm_pg = mx2.take("vm_pg", [P, 2, MT, D])
        q_mb = mx2.take("q_mb", [P, 2, KT, 32])
        assert mx2.at <= merged_at
        p_m = Region(o_at).take("p_m", [P, 2, QT, MEM])

        wo = Region(z_at)
        m2_hi = wo.take("m2_hi", [P, KT, T], F32R)
        m2_lo = wo.take("m2_lo", [P, KT, T], F32R)
        assert wo.at <= tail_at
        ff = Region(o_at)
        g_hi = ff.take("g_hi", [P, FT, T], F32R)
        g_lo = ff.take("g_lo", [P, FT, T], F32R)
        assert ff.at <= tail_at, (ff.at, tail_at)
        y_sb = Region(h_at).take("y_sb", [P, KT, T])
        acc = [ctx.enter_context(nc.psum_tensor(f"acc{u}", [P, 2, 512], F32)) for u in range(2)]
        ps4 = ctx.enter_context(nc.psum_tensor("ps4", [P, 4, 512], F32))

        def bank(n):
            return acc[n // 2][:, n % 2, :] if n < 4 else ps4[:, n - 4, :]

        def halves(x):
            return x.rearrange("p (c n) -> p c n", c=2)

        def acc_t(u):
            return acc[u][:, :, 0:HT]

        def view(ap, dims, skip=0):
            return bass.AP(tensor=ap.tensor, offset=ap.offset + skip, ap=[list(ap.ap[0])] + dims)

        def score_banks(h):
            return ps4[:, 0:2, :] if h % 2 else acc[1][:, :, :]

        def pv_bank(h):
            return 2 if h == MXH - 1 else 0

        def col(n, rows=P, w=1):
            return small[0:rows, n:n + w]

        ident = cst[:, C_ID:C_ID + P]
        sq_slot = (square[:, :], gate[:, :])
        n_slot = (scaled[:, 0, :], scaled[:, 1, :], gate[:, :], square[:, :])
        SUMS = (0, KT - 1, 2 * (KT - 1), 3 * KT - 2, 4 * KT - 2)

        LAM_AT = 511
        N_STAT, N_RS, N_HALF, N_LAM, N_LAMS = 0, 5, 10, 15, 18
        S_MAX, S_NEG, S_SUM, S_RC, S_SS, S_ST, S_R = range(20, 27)
        P_MAX, P_NEG, P_SUM, P_RC, P_SS, P_ST, P_R = 28, 32, 36, 40, 44, 52, 56
        M_NEG, M_SUM, M_RC = 64, 66, 68
        MP_NEG, MP_SUM, MP_RC = (70, 28), (74, 32), (78, 36)
        G_SS, G_ST, G_RS, N_SUBG = 82, 87, 92, 100

        def sem(name):
            return ctx.enter_context(nc.semaphore(name))

        def sems(name, n=2):
            return [sem(f"{name}{i}") for i in range(n)]

        w_loaded = sems("w_loaded")
        w_hi_done = sem("w_hi_done")
        w_lo_done = sem("w_lo_done")
        mm_done = sem("mm_done")
        acc_free = sems("acc_free")
        down_free = sems("down_free")
        x_loaded = sems("x_loaded", 4)
        sel_loaded = sem("sel_loaded")
        pages_loaded = sem("pages_loaded")
        cst_loaded = sem("cst_loaded")
        mem_loaded = sem("mem_loaded")
        sg_loaded = sem("sg_loaded")
        sgs_loaded = sem("sgs_loaded")
        const_set = sem("const_set")
        waits_passed = sem("waits_passed")
        v_zero = sem("v_zero")
        subg_ready = sem("subg_ready")
        lam_dot = sem("lam_dot")
        lam_exp = sem("lam_exp")
        lam_diff = sem("lam_diff")
        lam_neg = sem("lam_neg")
        lam_mm = sem("lam_mm")
        lam_ready = sem("lam_ready")
        line_mm = sem("line_mm")
        line_ready = sem("line_ready")
        line_stored = sem("line_stored")
        bias_skewed = sem("bias_skewed")
        bias_s_loaded = sem("bias_s_loaded")
        squared = sem("squared")
        summed = sem("summed")
        stat_mm = sem("stat_mm")
        stat_ready = sem("stat_ready")
        stat_pow = sem("stat_pow")
        diag_ready = sem("diag_ready")
        bcast_mm = sem("bcast_mm")
        rms_ready = sem("rms_ready")
        n_scaled = sem("n_scaled")
        n_hi = sem("n_hi")
        n_lo = sem("n_lo")
        n_lo_odd = sem("n_lo_odd")
        ssum_zero = sem("ssum_zero")
        y_ready = sem("y_ready")
        turned = sem("turned")
        nat_done = sem("nat_done")
        o_hi_done = sem("o_hi_done")
        o_lo_done = sem("o_lo_done")
        merged_done = sem("merged_done")
        ffn_hi = sem("ffn_hi")
        ffn_lo = sem("ffn_lo")
        ffn_silu = sem("ffn_silu")
        ffn_prod = sem("ffn_prod")
        stored = sem("stored")
        vs_stored = sem("vs_stored")
        y_stored = sem("y_stored")
        k_loaded = sems("k_loaded")
        x_again = sem("x_again")
        v_loaded = sem("v_loaded")
        v_late_loaded = sem("v_late_loaded")
        v_new_loaded = sem("v_new_loaded")
        s_q = sem("s_q")
        s_scores = sem("s_scores")
        s_logit = sem("s_logit")
        s_neg = sem("s_neg")
        s_exp = sem("s_exp")
        s_rc = sem("s_rc")
        s_coef = sem("s_coef")
        s_comb = sem("s_comb")
        s_aT = sem("s_aT")
        s_pv = sem("s_pv")
        s_masked = sem("s_masked")
        s_osum = sem("s_osum")
        s_oss = sem("s_oss")
        s_ost = sem("s_ost")
        s_orms = sem("s_orms")
        s_onorm = sem("s_onorm")
        s_oT = sem("s_oT")
        s_oout = sem("s_oout")
        p_bias = sems("p_bias")
        p_q = sem("p_q")
        p_zero = sem("p_zero")
        p_scores = sem("p_scores")
        p_logit = sem("p_logit")
        p_neg = sem("p_neg")
        p_exp = sem("p_exp")
        p_rc = sem("p_rc")
        p_a1 = sem("p_a1")
        p_a = sem("p_a")
        p_turn = sem("p_turn")
        p_aT = sem("p_aT")
        p_pv = sem("p_pv")
        p_oss = sem("p_oss")
        p_ost = sem("p_ost")
        p_orms = sem("p_orms")
        p_onorm = sem("p_onorm")
        p_oT = sem("p_oT")
        p_oout = sem("p_oout")
        g_ss = sem("g_ss")
        g_st = sem("g_st")
        g_rs = sem("g_rs")
        g_norm = sem("g_norm")
        g_wmask = sem("g_wmask")
        g_zero = sem("g_zero")
        g_slot = sem("g_slot")
        g_mix = sem("g_mix")
        g_bias = sem("g_bias")
        g_out = sem("g_out")
        km_loaded = sems("km_loaded")
        vm_loaded = sems("vm_loaded")
        m_zero = sem("m_zero")
        m_q = sem("m_q")
        m_scores = sem("m_scores")
        m_neg = sem("m_neg")
        m_exp = sem("m_exp")
        m_rc = sem("m_rc")
        m_p = sem("m_p")
        m_turn = sem("m_turn")
        m_pT = sem("m_pT")
        m_pv = sem("m_pv")
        m_masked = sem("m_masked")
        m_o = sem("m_o")
        m_oT = sem("m_oT")
        m_oout = sem("m_oout")
        c_scores = sem("c_scores")
        c_neg = sem("c_neg")
        c_exp = sem("c_exp")
        c_rc = sem("c_rc")
        c_p = sem("c_p")
        c_turn = sem("c_turn")
        c_pT = sem("c_pT")
        c_pv = sem("c_pv")
        c_oout = sem("c_oout")

        line_d = nc.dram_tensor("line_d", [HEADS, REV], F32, kind="Internal").ap()
        bias_sd = nc.dram_tensor("bias_sd", [HEADS, 2, TS, KEYS], F32, kind="Internal").ap()
        bias_pd = nc.dram_tensor("bias_pd", [HEADS, P, SEQ], F32, kind="Internal").ap()

        def wait(eng, s, value):
            if not isinstance(value, int) or value > 0:
                eng.wait_ge(s, value)

        def settle(eng, i):
            if not isinstance(i, int):
                eng.sem_inc(waits_passed, 1)

        def peeled(eng, n, body, first=1):
            for i in range(first):
                body(i)
            with eng.Fori(first, n) as i:
                body(i)

        def pairs(eng, body):
            body(0)
            with eng.Fori(1, HEADS // 2 - 1) as hp:
                body(hp)
            body(HEADS // 2 - 1, True)

        def all_evacuated(eng, stage):
            for u in range(2):
                eng.wait_ge(acc_free[u], FIRST[stage] // 2)

        block = ctx.enter_context(nc.Block())

        @block.sync
        def _(sp):
            def load_w(p, u):
                wait(sp, w_lo_done, p - 1)
                sp.dma_start(w_raw[:, u, :], w_stream[bass.ds(p, 1)].rearrange("a p n -> (a p) n"))\
                    .then_inc(w_loaded[u], 16)

            def stream(start, end):
                with sp.Fori(start // 2, end // 2) as i:
                    for u in range(2):
                        load_w(2 * i + u, u)

            def page_of(b):
                return [sp.value_load(pages[0:1, bass.ds(b * PAGES + j, 1)], min_val=0,
                                      max_val=cache_k.shape[0] - 1) for j in range(PAGES)]

            def key_pages(at, e):
                for j in range(PAGES):
                    sp.dma_start(k_slot[e][:, :, j * PAGE:(j + 1) * PAGE],
                                 cache_k[bass.ds(at[j], 1)].rearrange("a p (h n) -> (a p) h n", h=HEADS))\
                        .then_inc(k_loaded[e], 16)

            def value_pages(at, pg=v_pg, loaded=v_loaded):
                for j in range(PAGES):
                    sp.dma_start(pg[:, j, :], cache_v[bass.ds(at[j], 1)].rearrange("a p n -> (a p) n"))\
                        .then_inc(loaded, 16)

            def load_new_values(b):
                if isinstance(b, int):
                    sp.wait_ge(vs_stored, 16)
                sp.dma_start(v_new[0:TS, :], vs_out[bass.ds(b * TS, TS), :]).then_inc(v_new_loaded, 16)

            def load_keys_values(bk, bv, e):
                at_k, at_v = page_of(bk), page_of(bv)
                sp.wait_ge(s_scores, bk - 1)
                key_pages(at_k, e)
                sp.wait_ge(s_pv, bv)
                value_pages(at_v)
                load_new_values(bv)

            def load_x(c, loaded):
                sp.dma_start(x_sb[:, 2 * c:2 * c + 2, :], xT[2 * c * P:(2 * c + 2) * P, :]
                             .rearrange("(k p) n -> p k n", p=P)).then_inc(loaded, 16)

            for c in range(4):
                load_x(c, x_loaded[c])
                if c == 0:
                    sp.dma_start(cst[:, :], consts).then_inc(cst_loaded, 16)
                    sp.dma_start(par[:, :], params).then_inc(cst_loaded, 16)
            sp.dma_start(b_sel[:, :], bias_select).then_inc(sel_loaded, 16)
            for u in range(2):
                load_w(u, u)
            sp.dma_start(pages[:, :], page_table).then_inc(pages_loaded, 16)
            sp.wait_ge(line_ready, 2)
            sp.dma_start(line_d, rel_line[:, :]).then_inc(line_stored, 16)
            sp.wait_ge(line_stored, 16)
            for c in range(2):
                sp.dma_start(bias_sd[:, c], bass.AP(tensor=line_d.tensor, offset=TS - 1,
                                                    ap=[[REV, HEADS], [-1, TS], [1, KEYS]]))\
                    .then_inc(bias_skewed, 16)
            sp.dma_start(bias_pd, bass.AP(tensor=line_d.tensor, offset=KEYS - 1 - (SEQ - P),
                                          ap=[[REV, HEADS], [-1, P], [1, SEQ]])).then_inc(bias_skewed, 16)
            stream(2, FIRST["k"])
            sp.wait_ge(bias_skewed, 48)
            sp.wait_ge(pages_loaded, 16)
            sp.wait_ge(sel_loaded, 16)
            sp.dma_start(bias_s[:, :], bias_sd.rearrange("h c t k -> (h c t) k")).then_inc(bias_s_loaded, 16)
            key_pages(page_of(0), 0)
            stream(FIRST["k"], FIRST["v"])
            value_pages(page_of(0))
            stream(FIRST["v"], FIRST["v"] + 4)
            sp.wait_ge(n_lo, KT // 2)
            sp.wait_ge(n_lo_odd, KT // 2)
            key_pages(page_of(1), 1)
            stream(FIRST["v"] + 4, FIRST["da_branch"] + 2)

            third = page_of(2)
            sp.wait_ge(s_scores, 1)
            key_pages(third, 0)
            sp.wait_ge(v_zero, 1)
            load_new_values(0)
            with sp.Fori(0, 2) as i:
                load_keys_values(2 * i + 3, 2 * i + 1, 1)
                load_keys_values(2 * i + 4, 2 * i + 2, 0)
            at_k = page_of(NB - 1)
            sp.wait_ge(s_scores, NB - 2)
            key_pages(at_k, 1)
            at_v = page_of(NB - 3)
            sp.wait_ge(s_pv, NB - 3)
            value_pages(at_v)
            load_new_values(NB - 3)
            sp.wait_ge(s_scores, NB - 1)
            value_pages(page_of(NB - 2), v_late, v_late_loaded)
            at_v = page_of(NB - 1)
            sp.wait_ge(s_pv, NB - 2)
            load_new_values(NB - 2)
            value_pages(at_v)
            sp.wait_ge(s_pv, NB - 1)
            load_new_values(NB - 1)

            def load_bias(hp):
                for e in range(2):
                    if isinstance(hp, int):
                        sp.wait_ge(s_pv, NB - 1)
                    wait(sp, p_logit, 4 * (2 * hp + e - 1))
                    sp.dma_start(bias_p[:, e, :], bias_pd[bass.ds(2 * hp + e, 1)].rearrange("a p n -> (a p) n"))\
                        .then_inc(p_bias[e], 16)

            peeled(sp, HEADS // 2, load_bias)
            stream(FIRST["da_branch"] + 2, FIRST["s"])
            sp.wait_ge(o_lo_done, KT)
            sp.wait_ge(stored, 32)
            sp.dma_start(norm_b[:, :], bass.AP(tensor=sg_norm.tensor, offset=0, ap=[[0, P], [1, D]])).then_inc(sg_loaded, 16)
            sp.dma_start(sgb_b[:, :, :], bass.AP(tensor=sg_bias.tensor, offset=0, ap=[[0, P], [P, GROUPS], [1, P]])).then_inc(sg_loaded, 16)
            sp.dma_start(sg_w[:, :, :], sg_wT).then_inc(sg_loaded, 16)
            sp.wait_ge(g_zero, 1)
            for b in range(NB):
                sp.dma_start(sg_ws[b * TS:(b + 1) * TS, :, b * TS:(b + 1) * TS], sg_wT[0:TS, :, 0:TS],
                             allow_slow_non_contiguous=True).then_inc(sgs_loaded, 16)
            load_x(0, x_again)
            stream(FIRST["s"], FIRST["u"])
            load_x(1, x_again)
            stream(FIRST["u"], FIRST["sg_branch"])
            load_x(2, x_again)
            stream(FIRST["sg_branch"], FIRST["zm"])
            load_x(3, x_again)
            sp.wait_ge(o_lo_done, 2 * KT)
            sp.dma_start(m_x[:, :, :], memT.rearrange("(k p) n -> p k n", p=P)).then_inc(mem_loaded, 16)
            stream(FIRST["zm"], FIRST["mk"])
            sp.wait_ge(mm_done, FIRST["zm"])

            def mem_keys(b, e):
                wait(sp, m_scores, b - 1)
                sp.dma_start(km_pg[:, e], mem_k[bass.ds(b, 1)].rearrange("a p (f m) -> (a p) f m", f=KT))\
                    .then_inc(km_loaded[e], 16)

            def mem_values(b, e):
                wait(sp, m_pv, b - 1)
                sp.dma_start(vm_pg[:, e], mem_v[bass.ds(b, 1)].rearrange("a (m p) n -> (a p) m n", p=P))\
                    .then_inc(vm_loaded[e], 16)

            for e in range(2):
                mem_keys(e, e)
                mem_values(e, e)
            stream(FIRST["mk"], FIRST["mx_branch"] + 2)
            mem_keys(2, 0)
            with sp.Fori(1, NB // 2 - 1) as i:
                mem_keys(2 * i + 1, 1)
                mem_values(2 * i, 0)
                mem_keys(2 * i + 2, 0)
                mem_values(2 * i + 1, 1)
            mem_keys(NB - 1, 1)
            mem_values(NB - 2, 0)
            mem_values(NB - 1, 1)
            stream(FIRST["mx_branch"] + 2, PANELS)
            for k in range(KT):
                sp.wait_ge(y_ready, k + 1)
                sp.dma_start(yT[k * P:(k + 1) * P, :], y_sb[:, k, :]).then_inc(y_stored, 16)
            sp.wait_ge(y_stored, 16 * KT)
            sp.wait_ge(stored, 16 * 5)
            sp.wait_ge(vs_stored, 16)

        @block.scalar
        def _(act):
            def split_hi(p, u):
                act.wait_ge(w_loaded[u], 16 * (p // 2 + 1) if isinstance(p, int) else 8 * (p - u) + 16)
                wait(act, mm_done, p - 1)
                nc.scalar.activation(w_hi[:, u, :], w_raw[:, u, :], ACT.Copy).then_inc(w_hi_done, 1)

            def evacuate(p, u, out, func=ACT.Copy, scale=1.0, n=2):
                act.wait_ge(mm_done, p + 1)
                src = acc_t(u) if n == 2 else acc[u][:, 0, 0:MEM]
                nc.scalar.activation(out, src, func, scale=scale).then_inc(acc_free[u], 1)

            def norm_squares(x, n_cols, norm, x_ready=None):
                for k in range(KT):
                    if x_ready and k % 2 == 0:
                        act.wait_ge(x_ready[k // 2], 16)
                    if k >= 2:
                        act.wait_ge(summed, SUMS[norm] + max(1, k - 2))
                    nc.scalar.activation(sq_slot[k % 2][:, 0:n_cols], x[:, k, :], ACT.Square).then_inc(squared, 1)

            def rms_out(count, n_cols):
                act.wait_ge(bcast_mm, count + 1)
                if n_cols == T:
                    nc.scalar.activation(rms_b[:, 0:SEQ], bank(5), ACT.Copy)
                    nc.scalar.activation(rms_b[:, SEQ:T], bank(6)[:, 0:NS], ACT.Copy).then_inc(rms_ready, 1)
                else:
                    nc.scalar.activation(rms_b[:, 0:MEM], bank(5)[:, 0:MEM], ACT.Copy).then_inc(rms_ready, 1)

            def norm_hi(hi, n_cols, count):
                for k in range(KT):
                    act.wait_ge(n_scaled, count + k + 1)
                    nc.scalar.activation(hi[:, k, :], n_slot[k % 4][:, 0:n_cols], ACT.Copy).then_inc(n_hi, 1)

            def o_split(src, count, first=0, last=KT):
                for k in range(first, last):
                    nc.scalar.activation(o_hi[:, k, :], src[:, k, :], ACT.Copy).then_inc(o_hi_done, 1)

            norm_squares(x_sb, T, 0, x_loaded)
            act.wait_ge(cst_loaded, 32)
            act.wait_ge(const_set, 2)
            nc.scalar.activation(col(N_SUBG), par[:, G_SUB:G_SUB + 1], ACT.Copy, scale=1.0 - LAM_INIT)\
                .then_inc(subg_ready, 1)
            act.wait_ge(lam_dot, 2)
            nc.scalar.activation(lam_w[0:1, 2 * DK + 2:2 * DK + 4], lam_w[0:1, 2 * DK:2 * DK + 2], ACT.Exp)\
                .then_inc(lam_exp, 1)
            act.wait_ge(line_mm, 1)
            nc.scalar.activation(rel_line[:, 0:HREV], bank(7)[0:HEADS, 0:HREV], ACT.Copy).then_inc(line_ready, 1)
            nc.scalar.activation(rel_line[:, HREV:REV], bank(3)[0:HEADS, 0:HREV], ACT.Copy).then_inc(line_ready, 1)
            split_hi(0, 0)
            split_hi(1, 1)
            rms_out(0, T)
            norm_hi(h_hi, T, 0)

            for stage, dst, scale in (("q", qT, DK ** -0.5), ("k", kT, 1.0)):
                with act.Fori(0, 4) as i:
                    for u in range(2):
                        p = FIRST[stage] + 2 * i + u
                        evacuate(p, u, halves(dst[:, bass.ds(2 * i + u, 1), :].rearrange("p a n -> p (a n)")),
                                 scale=scale)
                        split_hi(p + 2, u)

            def turning(stage, count, func=ACT.Copy, n=2):
                def body(i):
                    for u in range(2):
                        p = FIRST[stage] + 2 * i + u
                        wait(act, turned, count + 2 * i + u - 1)
                        evacuate(p, u, halves(turn[:, u, :]) if n == 2 else turn[:, u, 0:MEM], func, n=n)
                        split_hi(p + 2, u)
                peeled(act, 4, body)

            turning("v", 0)

            def s_output(b):
                act.wait_ge(s_oT, b + 1)
                nc.scalar.activation(qT[:, :, bass.ds(SEQ + b * TS, TS)],
                                     bank(6)[:, 0:64].rearrange("p (h t) -> p h t", h=HEADS), ACT.Copy,
                                     scale=col(N_SUBG)).then_inc(s_oout, 1)

            def s_square(b):
                act.wait_ge(s_osum, b + 1)
                nc.scalar.activation(rms_b[0:64, 0:DV], o_s[:, 0, :], ACT.Square,
                                     accum_out=col(S_SS, 64)).then_inc(s_oss, 1)

            def s_body(i):
                for e in range(2):
                    b = 2 * i + e
                    if not isinstance(b, int) or b >= 3:
                        s_output(b - 3)
                    act.wait_ge(s_neg, b + 1)
                    nc.scalar.activation(logit_s[:, e, :], logit_s[:, e, :], ACT.Exp, bias=col(S_NEG),
                                         accum_out=col(S_SUM)).then_inc(s_exp, 1)
                    if not isinstance(b, int) or b >= 2:
                        s_square(b - 2)

            peeled(act, NB // 2, s_body, 2)
            s_output(NB - 3)
            s_square(NB - 2)
            s_output(NB - 2)
            s_square(NB - 1)

            def p_body(hp0, last_pair=False):
                def exps(n):
                    hp, n = hp0 + n // 8, n % 8
                    m, w = n % 2, (TILE_ORDER[n % 4] + 1) * P
                    act.wait_ge(p_neg, 8 * hp + n + 1)
                    for c in range(2):
                        last = nc.scalar.activation(logit_p[:, m, c, 0:w], logit_p[:, m, c, 0:w], ACT.Exp,
                                                    bias=col(P_NEG + 2 * m + c), accum_out=col(P_SUM + 2 * m + c))
                    last.then_inc(p_exp, 1)

                def turned_probs(n):
                    hp = hp0
                    m, w = n % 2, (TILE_ORDER[n % 4] + 1) * P
                    act.wait_ge(p_turn, 8 * hp + n + 1)
                    wait(act, p_pv, 8 * hp + n - 1)
                    nc.scalar.activation(aT_p[:, m, 0:w], bank(m)[:, 0:w], ACT.Copy).then_inc(p_aT, 1)

                def squares(e, hp):
                    act.wait_ge(p_pv, 8 * hp + 4 * e + 4)
                    for i in range(QT):
                        last = nc.scalar.activation(rms_b[:, i * DV:(i + 1) * DV], bank(2 + e)[:, i * DV:(i + 1) * DV], ACT.Square,
                                                    accum_out=col(P_SS + 4 * e + i))
                    last.then_inc(p_oss, 1)

                def output(e, hp):
                    act.wait_ge(p_oT, 2 * hp + e + 1)
                    nc.scalar.activation(qT[:, bass.ds(2 * hp + e, 1), 0:SEQ].rearrange("p a n -> p (a n)"),
                                         bank(2 + e), ACT.Copy, scale=col(N_SUBG)).then_inc(p_oout, 1)

                first_pair = isinstance(hp0, int) and hp0 == 0
                if first_pair:
                    exps(0)
                    s_output(NB - 1)
                for n in range(8):
                    if n < 7 or not last_pair:
                        exps(n + 1)
                    if n == 1 and not first_pair:
                        squares(1, hp0 - 1)
                    if n == 0 and not first_pair:
                        output(0, hp0 - 1)
                    if n == 4 and not first_pair:
                        output(1, hp0 - 1)
                    if n == 5:
                        squares(0, hp0)
                    turned_probs(n)
                if last_pair:
                    output(0, hp0)
                    squares(1, hp0)
                    act.wait_ge(p_oout, HEADS - 1)
                    o_split(qT, 0, 0, 5)
                    output(1, hp0)
                    act.wait_ge(p_oout, HEADS)
                    o_split(qT, 0, 5, KT)

            pairs(act, p_body)

            def branch(stage, then=None):
                def body(i):
                    p = FIRST[stage] + 2 * i
                    act.wait_ge(acc_free[1], FIRST[stage] // 2 + i)
                    evacuate(p, 0, halves(gate[:, :]), ACT.Sigmoid)
                    split_hi(p + 2, 0)
                    act.wait_ge(mm_done, p + 2)
                    split_hi(p + 3, 1)
                    if then:
                        then(i)
                with act.Fori(0, KT) as i:
                    body(i)

            branch("da_branch")

            turning("s", KT, ACT.Gelu_apprx_tanh)

            def u_tile(i, u):
                p = FIRST["u"] + 2 * i + u
                evacuate(p, u, halves(uT[:, bass.ds(2 * i + u, 1), :].rearrange("p a n -> p (a n)")),
                         ACT.Gelu_apprx_tanh)
                split_hi(p + 2, u)

            u_tile(0, 0)
            act.wait_ge(nat_done, 2 * KT)
            for j in range(QT + 1):
                rows = P if j < QT else NS
                last = nc.scalar.activation(nat_square[0:rows, j, :], s_nat[0:rows, j, :], ACT.Square,
                                            accum_out=col(G_SS + j, rows))
            last.then_inc(g_ss, 1)
            u_tile(0, 1)
            with act.Fori(1, 4) as i:
                for u in range(2):
                    u_tile(i, u)
            act.wait_ge(g_ss, 1)
            for k in range(KT):
                act.wait_ge(g_out, k + 1)
                nc.scalar.activation(o_hi[:, k, :], uT[:, k, :], ACT.Copy).then_inc(o_hi_done, 1)
            branch("sg_branch")

            act.wait_ge(stored, 48)
            act.wait_ge(mem_loaded, 16)
            act.wait_ge(acc_free[1], FIRST["zm"] // 2)
            norm_squares(m_x, MEM, 1)
            def zm_body(i):
                for u in range(2):
                    p = FIRST["zm"] + 2 * i + u
                    evacuate(p, u, halves(zmT[:, bass.ds(2 * i + u, 1), :].rearrange("p a n -> p (a n)")),
                             scale=MXD ** -0.5)
                    split_hi(p + 2, u)
            zm_body(0)
            zm_body(1)
            rms_out(1, MEM)
            norm_hi(m_hi, MEM, KT)
            with act.Fori(2, 4) as i:
                zm_body(i)
            with act.Fori(0, 4) as i:
                for u in range(2):
                    p = FIRST["mk"] + 2 * i + u
                    evacuate(p, u, kmT[:, bass.ds(2 * i + u, 1), :].rearrange("p a n -> p (a n)"), n=1)
                    split_hi(p + 2, u)
            turning("mv", 2 * KT, n=1)

            def m_output(b):
                act.wait_ge(m_oT, b + 1)
                out = zmT[:, :, bass.ds(SEQ + b * TS, TS)].rearrange("p (h f) t -> p f h t", f=2)
                for f in range(2):
                    last = nc.scalar.activation(out[:, f], bank(7)[:, f * 32:f * 32 + 32]
                                                .rearrange("p (h t) -> p h t", h=MXH), ACT.Copy)
                last.then_inc(m_oout, 1)

            def m_body(i):
                for e in range(2):
                    b = 2 * i + e
                    act.wait_ge(m_neg, b + 1)
                    nc.scalar.activation(p_mb[:, e, :], bank(4 + e)[0:32, 0:MEM], ACT.Exp,
                                         bias=col(M_NEG + e, 32), accum_out=col(M_SUM + e, 32)).then_inc(m_exp, 1)
                    if not isinstance(i, int):
                        m_output(b - 2)
                    act.wait_ge(m_turn, b + 1)
                    wait(act, m_pv, b - 1)
                    nc.scalar.activation(pT_mb[:, e, :], bank(6)[:, 0:MT * 32], ACT.Copy).then_inc(m_pT, 1)

            peeled(act, NB // 2, m_body)
            m_output(NB - 2)

            def c_exps(h):
                m = h % 2
                act.wait_ge(c_neg, h + 1)
                wait(act, c_turn, h - 1)
                for i in range(QT):
                    last = nc.scalar.activation(p_m[:, m, i, :], score_banks(h)[:, i // 2, (i % 2) * MEM:(i % 2 + 1) * MEM],
                                                ACT.Exp, bias=col(MP_NEG[m] + i), accum_out=col(MP_SUM[m] + i))
                last.then_inc(c_exp, 1)

            def c_turned(h):
                act.wait_ge(c_turn, h + 1)
                wait(act, c_pv, h)
                for m in range(MT):
                    last = nc.scalar.activation(pT_m[:, m, :], bank(6 + m), ACT.Copy)
                last.then_inc(c_pT, 1)

            def c_output(h):
                act.wait_ge(c_pv, h + 1)
                for f in range(2):
                    last = nc.scalar.activation(zmT[:, 2 * h + f, 0:SEQ], bank(pv_bank(h) + f), ACT.Copy)
                last.then_inc(c_oout, 1)

            c_exps(0)
            m_output(NB - 1)
            for h in range(MXH):
                if h < MXH - 1:
                    c_exps(h + 1)
                if h > 0:
                    c_output(h - 1)
                c_turned(h)
            act.wait_ge(c_oout, MXH - 1)
            o_split(zmT, 2 * KT, 0, KT - 2)
            c_output(MXH - 1)
            act.wait_ge(c_oout, MXH)
            o_split(zmT, 2 * KT, KT - 2, KT)

            def merged_hi(i):
                act.wait_ge(merged_done, KT + i + 1)
                nc.scalar.activation(m2_hi[:, bass.ds(i, 1), :].rearrange("p a n -> p (a n)"),
                                     merged[:, bass.ds(i, 1), :].rearrange("p a n -> p (a n)"), ACT.Copy)\
                    .then_inc(o_hi_done, 1)
            branch("mx_branch", merged_hi)

            def resid_square(n, u, norm):
                act.wait_ge(summed, SUMS[norm] + n - 1)
                nc.scalar.activation(sq_slot[u], x_sb[:, bass.ds(n, 1), :].rearrange("p a n -> p (a n)"),
                                     ACT.Square).then_inc(squared, 1)

            with act.Fori(0, 4) as i:
                for u in range(2):
                    p = FIRST["w_out"] + 2 * i + u
                    act.wait_ge(mm_done, p + 1)
                    split_hi(p + 2, u)
                    act.wait_ge(acc_free[u], FIRST["w_out"] // 2 + i + 1)
                    resid_square(2 * i + u, u, 2)
                    act.wait_ge(n_scaled, 2 * KT + 2 * i + u + 1)
                    nc.scalar.activation(h_hi[:, bass.ds(2 * i + u, 1), :].rearrange("p a n -> p (a n)"),
                                         scaled[:, u, :], ACT.Copy).then_inc(n_hi, 1)

            def up_body(i):
                p = FIRST["up"] + 2 * i
                act.wait_ge(mm_done, p + 1)
                split_hi(p + 2, 0)
                if isinstance(i, int):
                    rms_out(2, T)
                act.wait_ge(mm_done, p + 2)
                split_hi(p + 3, 1)
                act.wait_ge(acc_free[0], FIRST["up"] // 2 + i + 1)
                nc.scalar.activation(gate[:, :], scaled[:, 0, :], ACT.Silu).then_inc(ffn_silu, 1)
                act.wait_ge(ffn_prod, i + 1)
                nc.scalar.activation(g_hi[:, bass.ds(i, 1), :].rearrange("p a n -> p (a n)"), scaled[:, 1, :],
                                     ACT.Copy).then_inc(ffn_hi, 1)
            peeled(act, FT, up_body)

            def down_body(i):
                for f in range(2):
                    for c in range(3):
                        q = 3 * f + c
                        p = FIRST["down"] + 6 * i + q
                        if isinstance(i, int) and p + 2 >= PANELS:
                            continue
                        act.wait_ge(mm_done, p + 1)
                        split_hi(p + 2, q % 2)
                    act.wait_ge(down_free[f], i + 1)
                    resid_square(2 * i + f, f, 3)
            with act.Fori(0, 3) as i:
                down_body(i)
            down_body(3)
            rms_out(3, T)

        @block.vector
        def _(dve):
            def split_lo(p, u):
                dve.wait_ge(w_hi_done, p + 1)
                nc.vector.tensor_tensor(w_lo[:, u, :], w_raw[:, u, :], w_hi[:, u, :].bitcast(F32), ALU.subtract)\
                    .then_inc(w_lo_done, 1)

            def norm_stats(count, n_cols):
                nt = 5 if n_cols == T else 2
                dve.wait_ge(stat_mm, count + 1)
                nc.vector.tensor_scalar(col(N_STAT, w=nt), bank(4)[:, 0:nt], EPS, None, ALU.add)\
                    .then_inc(stat_ready, 1)
                dve.wait_ge(stat_pow, count + 1)
                for j in range(nt):
                    last = nc.vector.tensor_scalar(diag[:, j, :], ident, col(N_RS + j), None, ALU.mult)
                last.then_inc(diag_ready, 1)

            def norm_sum(norm, n_cols):
                for k in range(1, KT):
                    dve.wait_ge(squared, norm * KT + k + 1)
                    if k >= 2:
                        dve.wait_ge(summed, SUMS[norm] + k - 1)
                    nc.vector.tensor_tensor(ssum[:, 0:n_cols], sq_slot[0][:, 0:n_cols] if k == 1 else ssum[:, 0:n_cols],
                                            sq_slot[k % 2][:, 0:n_cols], ALU.add).then_inc(summed, 1)

            def norm_split(x, lo, hi, gain, n_cols, norm):
                def scale(k):
                    if k >= 4:
                        dve.wait_ge(n_lo if k % 2 == 0 else n_lo_odd, norm * 4 + (k - 4) // 2 + 1)
                    nc.vector.scalar_tensor_tensor(n_slot[k % 4][:, 0:n_cols], x[:, k, :],
                                                   par[:, gain + k:gain + k + 1], rms_b[:, 0:n_cols],
                                                   ALU.mult, ALU.mult).then_inc(n_scaled, 1)

                def low(k):
                    dve.wait_ge(n_hi, norm * KT + k + 1)
                    nc.vector.tensor_tensor(lo[:, k, :], n_slot[k % 4][:, 0:n_cols], hi[:, k, :].bitcast(F32),
                                            ALU.subtract).then_inc(n_lo, 1)
                dve.wait_ge(rms_ready, norm + 1)
                for k in range(KT):
                    scale(k)
                    if k % 2 == 0 and k > 0:
                        low(k - 2)
                low(KT - 2)

            def add_square(n, u, norm):
                dve.wait_ge(squared, norm * KT + n + 1)
                dve.wait_ge(summed, SUMS[norm] + n)
                nc.vector.tensor_tensor(ssum[:, :], ssum[:, :], sq_slot[u], ALU.add).then_inc(summed, 1)

            dve.wait_ge(cst_loaded, 32)
            for c in range(2):
                nc.vector.tensor_tensor_reduce(out=lam_w[0:1, c * DK:(c + 1) * DK],
                                               in0=par[0:1, G_LAM + 2 * c * DK:G_LAM + (2 * c + 1) * DK],
                                               in1=par[0:1, G_LAM + (2 * c + 1) * DK:G_LAM + (2 * c + 2) * DK],
                                               scale=1.0, scalar=0.0, op0=ALU.mult, op1=ALU.add,
                                               accum_out=lam_w[0:1, 2 * DK + c:2 * DK + c + 1]).then_inc(lam_dot, 1)
            norm_sum(0, T)
            dve.wait_ge(lam_exp, 1)
            nc.vector.tensor_tensor(lam_w[0:1, 2 * DK + 4:2 * DK + 5], lam_w[0:1, 2 * DK + 3:2 * DK + 4],
                                    lam_w[0:1, 2 * DK + 2:2 * DK + 3], ALU.subtract).then_inc(lam_diff, 1)
            dve.wait_ge(lam_diff, 1)
            nc.vector.tensor_scalar(lam_w[0:1, 2 * DK + 5:2 * DK + 6], lam_w[0:1, 2 * DK + 4:2 * DK + 5],
                                    LAM_INIT, None, ALU.subtract).then_inc(lam_neg, 1)
            norm_stats(0, T)
            split_lo(0, 0)
            split_lo(1, 1)
            norm_split(x_sb, h_lo, h_hi, G_ATTN, T, 0)
            dve.wait_ge(lam_mm, 1)
            nc.vector.tensor_copy(col(N_LAM), bank(7)[:, LAM_AT:LAM_AT + 1]).then_inc(lam_ready, 1)
            dve.wait_ge(lam_ready, 1)
            nc.vector.tensor_scalar(col(N_LAMS), cst[:, C_C1:C_C1 + 1], col(N_LAM), None, ALU.mult)\
                .then_inc(lam_ready, 1)
            dve.wait_ge(lam_ready, 2)
            nc.vector.scalar_tensor_tensor(col(N_LAMS), cst[:, C_C1:C_C1 + 1], -1.0, col(N_LAMS), ALU.mult, ALU.add)\
                .then_inc(lam_ready, 1)
            dve.wait_ge(lam_ready, 3)
            nc.vector.tensor_scalar(col(N_LAMS), col(N_LAMS), 1.0, None, ALU.add).then_inc(lam_ready, 1)

            def lows(stage, pairs=4):
                with dve.Fori(0, pairs) as i:
                    for u in range(2):
                        split_lo(FIRST[stage] + 2 * i + u + 2, u)

            def turning(stage, nat, count, sampled=True):
                with dve.Fori(0, 4) as i:
                    for u in range(2):
                        n = 2 * i + u
                        split_lo(FIRST[stage] + n + 2, u)
                        dve.wait_ge(turned, count + n + 1)
                        nt = QT if sampled else MT
                        last = nc.vector.tensor_copy(nat[:, 0:nt, bass.ds(n * P, P)],
                                                     bank(4 + u)[:, 0:nt * P].rearrange("p (j d) -> p j d", j=nt))
                        if sampled:
                            last = nc.vector.tensor_copy(nat[0:NS, QT, bass.ds(n * P, P)], bank(6 + u)[0:NS, 0:P])
                        last.then_inc(nat_done, 1)

            lows("q")
            lows("k")
            turning("v", v_nat, 0)

            def s_heads(b):
                dve.wait_ge(s_pv, b + 1)
                nc.vector.tensor_tensor(masked_s[:, :].rearrange("p (h d) -> p h d", h=HEADS),
                                        ps4[0:64, 0:2, :].rearrange("p a (h d) -> p (a h) d", d=DV),
                                        cst[0:64, C_M8:C_M8 + 8].unsqueeze(2).to_broadcast([64, HEADS, DV]),
                                        ALU.mult).then_inc(s_masked, 1)

            def s_reduce(b):
                dve.wait_ge(s_masked, b + 1)
                nc.vector.tensor_reduce(o_s[:, 0, :], masked_s[:, :].rearrange("p (h d) -> p d h", h=HEADS),
                                        AX.X, ALU.add).then_inc(s_osum, 1)

            def s_norm(b):
                dve.wait_ge(s_orms, b + 1)
                wait(dve, s_oT, b)
                nc.vector.tensor_scalar(o_s[:, 1, :], o_s[:, 0, :], col(S_R, 64), None, ALU.mult)\
                    .then_inc(s_onorm, 1)

            def s_combined(b):
                dve.wait_ge(s_comb, b + 1)
                wait(dve, s_pv, b)
                nc.vector.tensor_copy(aT_s[:, 0:PAGES * 64], bank(2)[:, 0:PAGES * 64])
                nc.vector.tensor_copy(aT_s[0:TS, PAGES * 64:], bank(3)[0:TS, 0:64]).then_inc(s_aT, 1)

            def s_body(i):
                for e in range(2):
                    b = 2 * i + e
                    dve.wait_ge(s_scores, b + 1)
                    wait(dve, s_comb, b - 1)
                    settle(dve, b)
                    nc.vector.tensor_tensor_reduce(out=logit_s[:, e, :].rearrange("p (c n) -> p c n", c=2),
                                                   in0=acc[0][:, :, 0:HK],
                                                   in1=bias_s[:, :].rearrange("p (c n) -> p c n", c=2),
                                                   scale=1.0, scalar=NEG, op0=ALU.add, op1=ALU.max,
                                                   accum_out=col(S_MAX)).then_inc(s_logit, 1)
                    dve.wait_ge(s_logit, b + 1)
                    nc.vector.tensor_scalar(col(S_NEG), col(S_MAX), -1.0, None, ALU.mult).then_inc(s_neg, 1)
                    if not isinstance(b, int) or b >= 2:
                        s_heads(b - 2)
                    if not isinstance(b, int) or b >= 1:
                        s_combined(b - 1)
                    if not isinstance(b, int) or b >= 2:
                        s_reduce(b - 2)
                    dve.wait_ge(s_exp, b + 1)
                    nc.vector.reciprocal(col(S_RC), col(S_SUM)).then_inc(s_rc, 1)
                    dve.wait_ge(s_rc, b + 1)
                    nc.vector.tensor_scalar(coef_s[:, :], cst[:, C_COMB:C_COMB + 64], col(S_RC), col(N_LAMS),
                                            ALU.mult, ALU.mult).then_inc(s_coef, 1)
                    if not isinstance(b, int) or b >= 2:
                        s_norm(b - 2)

            dve.wait_ge(v_zero, 2)
            dve.wait_ge(bias_s_loaded, 16)
            dve.wait_ge(lam_ready, 4)
            peeled(dve, NB // 2, s_body, 2)
            s_heads(NB - 2)
            s_combined(NB - 1)
            s_reduce(NB - 2)
            s_norm(NB - 2)
            s_heads(NB - 1)
            s_reduce(NB - 1)

            def p_body(hp0, last_pair=False):
                def logits(n):
                    hp, n = hp0 + n // 8, n % 8
                    m, e, w = n % 2, n // 4, (TILE_ORDER[n % 4] + 1) * P
                    dve.wait_ge(p_scores, 8 * hp + n + 1)
                    if n % 4 == 0:
                        dve.wait_ge(p_bias[e], 16 * hp + 16)
                    wait(dve, p_a, 8 * hp + n - 1)
                    settle(dve, hp)
                    for c in range(2):
                        last = nc.vector.tensor_tensor_reduce(
                            out=logit_p[:, m, c, 0:w], in0=bank(4 + 2 * m + c)[:, 0:w],
                            in1=bias_p[:, e, SEQ - w:SEQ], scale=1.0, scalar=NEG, op0=ALU.add, op1=ALU.max,
                            accum_out=col(P_MAX + 2 * m + c))
                    last.then_inc(p_logit, 1)
                    dve.wait_ge(p_logit, 8 * hp + n + 1)
                    nc.vector.tensor_scalar(col(P_NEG + 2 * m, w=2), col(P_MAX + 2 * m, w=2), -1.0, None, ALU.mult)\
                        .then_inc(p_neg, 1)

                def combine(n):
                    hp = hp0
                    m, w = n % 2, (TILE_ORDER[n % 4] + 1) * P
                    dve.wait_ge(p_exp, 8 * hp + n + 1)
                    nc.vector.reciprocal(col(P_RC + 2 * m, w=2), col(P_SUM + 2 * m, w=2)).then_inc(p_rc, 1)
                    dve.wait_ge(p_rc, 8 * hp + n + 1)
                    wait(dve, p_turn, 8 * hp + n - 1)
                    nc.vector.tensor_scalar(a_p[:, m, 0:w], logit_p[:, m, 1, 0:w], col(P_RC + 2 * m + 1), col(N_LAM),
                                            ALU.mult, ALU.mult).then_inc(p_a1, 1)
                    dve.wait_ge(p_a1, 8 * hp + n + 1)
                    nc.vector.scalar_tensor_tensor(a_p[:, m, 0:w], logit_p[:, m, 0, 0:w], col(P_RC + 2 * m),
                                                   a_p[:, m, 0:w], ALU.mult, ALU.add).then_inc(p_a, 1)

                def norm(e, hp):
                    dve.wait_ge(p_orms, 2 * hp + e + 1)
                    nc.vector.tensor_tensor(o_p[:, e, :].rearrange("p (i d) -> p i d", i=QT),
                                            bank(2 + e).rearrange("p (i d) -> p i d", i=QT),
                                            col(P_R + 4 * e, w=4).unsqueeze(2).to_broadcast([P, QT, DV]),
                                            ALU.mult).then_inc(p_onorm, 1)

                first_pair = isinstance(hp0, int) and hp0 == 0
                if first_pair:
                    logits(0)
                    s_norm(NB - 1)
                for n in range(8):
                    if n < 7 or not last_pair:
                        logits(n + 1)
                    combine(n)
                    if n == 2 and not first_pair:
                        norm(1, hp0 - 1)
                    if n == 6:
                        norm(0, hp0)
                if last_pair:
                    norm(1, hp0)

            pairs(dve, p_body)

            def o_split(src, count):
                for k in range(KT):
                    dve.wait_ge(o_hi_done, count + k + 1)
                    nc.vector.tensor_tensor(o_lo[:, k, :], src[:, k, :], o_hi[:, k, :].bitcast(F32), ALU.subtract)\
                        .then_inc(o_lo_done, 1)

            def branch(stage, first_branch=False, then=None):
                def body(i):
                    p = FIRST[stage] + 2 * i
                    split_lo(p + 2, 0)
                    split_lo(p + 3, 1)
                    dve.wait_ge(mm_done, p + 2)
                    dve.wait_ge(acc_free[0], FIRST[stage] // 2 + i + 1)
                    into = merged[:, bass.ds(i, 1), :].rearrange("p a n -> p (a n)")
                    if first_branch:
                        nc.vector.tensor_tensor(halves(into), acc_t(1), halves(gate[:, :]), ALU.mult)\
                            .then_inc(acc_free[1], 1)
                    else:
                        dve.wait_ge(w_lo_done, p + 4)
                        nc.vector.tensor_tensor(halves(scaled[:, 0, :]), acc_t(1), halves(gate[:, :]), ALU.mult)\
                            .then_inc(acc_free[1], 1)
                        dve.wait_ge(acc_free[1], FIRST[stage] // 2 + i + 1)
                        nc.vector.tensor_tensor(into, into, scaled[:, 0, :], ALU.add).then_inc(merged_done, 1)
                    if then:
                        then(i)
                with dve.Fori(0, KT) as i:
                    body(i)

            o_split(qT, 0)
            branch("da_branch", True)

            turning("s", s_nat, KT)
            def gate_mix(n, u):
                dve.wait_ge(g_mix, n + 1)
                dve.wait_ge(acc_free[u], (FIRST["u"] + n) // 2 + 1 if isinstance(n, int)
                            else FIRST["u"] // 2 + (n - u) // 2 + 1)
                wait(dve, g_out, n)
                bias = sgb_b[:, bass.ds(n, 1), :]
                nc.vector.tensor_tensor(mixed[:, 0:SEQ].rearrange("p (j d) -> p j d", j=QT),
                                        bank(4 + u).rearrange("p (j d) -> p j d", j=QT),
                                        bias.to_broadcast([P, QT, P]), ALU.add)
                nc.vector.tensor_tensor(mixed[:, SEQ:T].rearrange("p (b t) -> p b t", b=NB),
                                        bank(6 + u)[:, 0:NS].rearrange("p (b t) -> p b t", b=NB),
                                        bias[:, :, 0:TS].to_broadcast([P, NB, TS]), ALU.add).then_inc(g_bias, 1)
                dve.wait_ge(g_bias, n + 1)
                into = uT[:, bass.ds(n, 1), :].rearrange("p a n -> p (a n)")
                nc.vector.tensor_tensor(into, into, mixed[:, :], ALU.mult).then_inc(g_out, 1)

            def u_body(i):
                for u in range(2):
                    split_lo(FIRST["u"] + 2 * i + u + 2, u)
                    if not isinstance(i, int) or i and u:
                        gate_mix(2 * i + u - 3, 1 - u)

            u_body(0)
            dve.wait_ge(g_rs, 1)
            dve.wait_ge(sg_loaded, 48)
            for j in range(QT + 1):
                rows = P if j < QT else NS
                last = nc.vector.scalar_tensor_tensor(s_nat[0:rows, j, :], s_nat[0:rows, j, :], col(G_RS + j, rows),
                                                      norm_b[0:rows, :], ALU.mult, ALU.mult)
            last.then_inc(g_norm, 1)
            u_body(1)
            with dve.Fori(2, 4) as i:
                u_body(i)
            for n in range(KT - 3, KT):
                gate_mix(n, n % 2)
            o_split(uT, KT)
            branch("sg_branch")

            def zm_body(i):
                for u in range(2):
                    split_lo(FIRST["zm"] + 2 * i + u + 2, u)
            norm_sum(1, MEM)
            zm_body(0)
            norm_stats(1, MEM)
            zm_body(1)
            norm_split(m_x, m_lo, m_hi, G_MEM, MEM, 1)
            with dve.Fori(2, 4) as i:
                zm_body(i)
            lows("mk")
            turning("mv", vm_nat, 2 * KT, sampled=False)

            def m_out(b, e):
                dve.wait_ge(m_pv, b + 1)
                nc.vector.tensor_tensor(masked_m[:, :].rearrange("p (h d) -> p h d", h=MXH),
                                        acc[0][0:32, :, :].rearrange("p a (h d) -> p (a h) d", d=MXD),
                                        cst[0:32, C_M4:C_M4 + 4].unsqueeze(2).to_broadcast([32, MXH, MXD]),
                                        ALU.mult).then_inc(m_masked, 1)
                dve.wait_ge(m_masked, b + 1)
                wait(dve, m_oT, b - 1)
                nc.vector.tensor_reduce(o_m[:, e, :], masked_m[:, :].rearrange("p (h d) -> p d h", h=MXH),
                                        AX.X, ALU.add).then_inc(m_o, 1)

            def m_body(i):
                for e in range(2):
                    b = 2 * i + e
                    dve.wait_ge(m_scores, b + 1)
                    nc.vector.tensor_reduce(col(M_NEG + e, 32), bank(4 + e)[0:32, 0:MEM], AX.X, ALU.max, negate=True)\
                        .then_inc(m_neg, 1)
                    dve.wait_ge(m_exp, b + 1)
                    nc.vector.reciprocal(col(M_RC + e, 32), col(M_SUM + e, 32)).then_inc(m_rc, 1)
                    dve.wait_ge(m_rc, b + 1)
                    nc.vector.tensor_scalar(p_mb[:, e, :], p_mb[:, e, :], col(M_RC + e, 32), None, ALU.mult)\
                        .then_inc(m_p, 1)
                    if not isinstance(i, int) or e:
                        m_out(b - 1, 1 - e)
            peeled(dve, NB // 2, m_body)
            m_out(NB - 1, 1)

            def c_max(h):
                dve.wait_ge(c_scores, h + 1)
                nc.vector.tensor_reduce(col(MP_NEG[h % 2], w=QT), score_banks(h).rearrange("p a (i m) -> p (a i) m", m=MEM),
                                        AX.X, ALU.max, negate=True).then_inc(c_neg, 1)

            def c_scale(h):
                m = h % 2
                dve.wait_ge(c_exp, h + 1)
                nc.vector.reciprocal(col(MP_RC[m], w=QT), col(MP_SUM[m], w=QT)).then_inc(c_rc, 1)
                dve.wait_ge(c_rc, h + 1)
                nc.vector.tensor_tensor(p_m[:, m], p_m[:, m], col(MP_RC[m], w=QT).unsqueeze(2).to_broadcast([P, QT, MEM]),
                                        ALU.mult).then_inc(c_p, 1)
            for h in range(MXH):
                c_max(h)
                c_scale(h)

            o_split(zmT, 2 * KT)
            dve.wait_ge(stored, 80)

            def merged_lo(i):
                dve.wait_ge(o_hi_done, 3 * KT + i + 1)
                nc.vector.tensor_tensor(m2_lo[:, bass.ds(i, 1), :].rearrange("p a n -> p (a n)"),
                                        merged[:, bass.ds(i, 1), :].rearrange("p a n -> p (a n)"),
                                        m2_hi[:, bass.ds(i, 1), :].rearrange("p a n -> p (a n)").bitcast(F32),
                                        ALU.subtract).then_inc(o_lo_done, 1)
            branch("mx_branch", then=merged_lo)

            nc.vector.memset(ssum[:, :], 0.0).then_inc(ssum_zero, 1)
            dve.wait_ge(ssum_zero, 1)
            dve.wait_ge(merged_done, 2 * KT)
            dve.wait_ge(x_again, 64)
            with dve.Fori(0, 4) as i:
                for u in range(2):
                    n = 2 * i + u
                    p = FIRST["w_out"] + n
                    split_lo(p + 2, u)
                    dve.wait_ge(mm_done, p + 1)
                    x_tile = x_sb[:, bass.ds(n, 1), :].rearrange("p a n -> p (a n)")
                    nc.vector.tensor_tensor(halves(x_tile), acc_t(u), halves(x_tile), ALU.add).then_inc(acc_free[u], 1)
                    dve.wait_ge(acc_free[u], FIRST["w_out"] // 2 + i + 1)
                    dve.wait_ge(n_lo, KT + n - 1)
                    nc.vector.tensor_tensor(scaled[:, u, :], x_tile,
                                            par[:, bass.ds(n + G_FFN, 1)].to_broadcast([P, T]), ALU.mult)\
                        .then_inc(n_scaled, 1)
                    add_square(n, u, 2)
                    dve.wait_ge(n_hi, 2 * KT + n + 1)
                    nc.vector.tensor_tensor(h_lo[:, bass.ds(n, 1), :].rearrange("p a n -> p (a n)"), scaled[:, u, :],
                                            h_hi[:, bass.ds(n, 1), :].rearrange("p a n -> p (a n)").bitcast(F32),
                                            ALU.subtract).then_inc(n_lo, 1)
            norm_stats(2, T)
            dve.wait_ge(n_lo, 2 * KT)

            def up_body(i):
                p = FIRST["up"] + 2 * i
                split_lo(p + 2, 0)
                if isinstance(i, int):
                    dve.wait_ge(rms_ready, 3)
                dve.wait_ge(mm_done, p + 1)
                nc.vector.tensor_tensor(halves(scaled[:, 0, :]), acc_t(0), halves(rms_b[:, :]), ALU.mult)\
                    .then_inc(acc_free[0], 1)
                split_lo(p + 3, 1)
                dve.wait_ge(mm_done, p + 2)
                wait(dve, ffn_lo, i)
                nc.vector.tensor_tensor(halves(scaled[:, 1, :]), acc_t(1), halves(rms_b[:, :]), ALU.mult)\
                    .then_inc(acc_free[1], 1)
                dve.wait_ge(acc_free[1], FIRST["up"] // 2 + i + 1)
                dve.wait_ge(ffn_silu, i + 1)
                nc.vector.tensor_tensor(scaled[:, 1, :], scaled[:, 1, :], gate[:, :], ALU.mult).then_inc(ffn_prod, 1)
                dve.wait_ge(ffn_hi, i + 1)
                nc.vector.tensor_tensor(g_lo[:, bass.ds(i, 1), :].rearrange("p a n -> p (a n)"), scaled[:, 1, :],
                                        g_hi[:, bass.ds(i, 1), :].rearrange("p a n -> p (a n)").bitcast(F32),
                                        ALU.subtract).then_inc(ffn_lo, 1)
            peeled(dve, FT, up_body)
            nc.vector.memset(ssum[:, :], 0.0).then_inc(ssum_zero, 1)
            dve.wait_ge(ssum_zero, 2)

            def down_body(i):
                for f in range(2):
                    for c in range(3):
                        q = 3 * f + c
                        p = FIRST["down"] + 6 * i + q
                        if isinstance(i, int) and p + 2 >= PANELS:
                            continue
                        split_lo(p + 2, q % 2)
                    dve.wait_ge(mm_done, FIRST["down"] + 6 * i + 3 * f + 3)
                    into = halves(x_sb[:, bass.ds(2 * i + f, 1), :].rearrange("p a n -> p (a n)"))
                    nc.vector.tensor_tensor(into, acc_t(f), into, ALU.add).then_inc(down_free[f], 1)
                    add_square(2 * i + f, f, 3)
            with dve.Fori(0, 3) as i:
                down_body(i)
            down_body(3)
            norm_stats(3, T)
            dve.wait_ge(rms_ready, 4)
            for k in range(KT):
                nc.vector.scalar_tensor_tensor(y_sb[:, k, :], x_sb[:, k, :], par[:, G_FINAL + k:G_FINAL + k + 1],
                                               rms_b[:, :], ALU.mult, ALU.mult).then_inc(y_ready, 1)

        @block.gpsimd
        def _(pool):
            def norm_pow(count, n_cols):
                nt = 5 if n_cols == T else 2
                pool.wait_ge(stat_ready, count + 1)
                nc.gpsimd.tensor_tensor(col(N_RS, w=nt), col(N_STAT, w=nt), col(N_HALF, w=nt), ALU.pow)\
                    .then_inc(stat_pow, 1)

            def norm_lo(lo, hi, n_cols, count):
                for k in range(1, KT, 2):
                    pool.wait_ge(n_hi, count + k + 1)
                    nc.gpsimd.tensor_tensor(lo[:, k, :], n_slot[k % 4][:, 0:n_cols], hi[:, k, :].bitcast(F32),
                                            ALU.subtract).then_inc(n_lo_odd, 1)

            nc.gpsimd.memset(small[:, :], 1.0).then_inc(const_set, 1)
            pool.wait_ge(const_set, 1)
            nc.gpsimd.memset(col(N_HALF, w=5), -0.5).then_inc(const_set, 1)
            nc.gpsimd.memset(q_blk[:, :, :], 0.0).then_inc(const_set, 1)
            norm_pow(0, T)
            norm_lo(h_lo, h_hi, T, 0)
            pool.wait_ge(n_lo_odd, 4)
            nc.gpsimd.memset(v_new[:, :], 0.0).then_inc(v_zero, 1)
            nc.gpsimd.memset(aT_s[:, PAGES * 64:], 0.0).then_inc(v_zero, 1)

            pool.wait_ge(acc_free[0], FIRST["v"] // 2)
            pool.wait_ge(acc_free[1], FIRST["v"] // 2)
            pool.dma_start(kT_out.rearrange("(k p) n -> p k n", p=P), kT[:, :, :]).then_inc(stored, 16)
            def s_queries(b, e):
                wait(pool, s_scores, b)
                wait(pool, s_q, 3 * b)
                nc.gpsimd.tensor_copy(k_slot[e][:, :, PAST:KEYS], kT[:, :, bass.ds(SEQ + b * TS, TS)]).then_inc(s_q, 1)
                for c in range(2):
                    rows = slice(c * DK, (c + 1) * DK)
                    if c == 1:
                        pool.wait_ge(s_q, 3 * b + 2)
                    nc.gpsimd.tensor_copy(view(q_blk[rows, 0, :], [[P + 2 * TS, HEADS], [1, TS]], c * TS),
                                          qT[rows, :, bass.ds(SEQ + b * TS, TS)]).then_inc(s_q, 1)

            pool.wait_ge(const_set, 3)
            pool.wait_ge(v_zero, 2)
            s_queries(0, 0)
            s_queries(1, 1)
            pool.wait_ge(nat_done, KT)
            pool.dma_start(vs_out, v_nat[0:NS, QT, :]).then_inc(vs_stored, 16)
            s_queries(2, 0)
            pool.dma_start(v_out.rearrange("(j p) n -> p j n", p=P), v_nat[:, 0:QT, :]).then_inc(stored, 16)

            def s_power(b):
                pool.wait_ge(s_oss, b + 1)
                settle(pool, b)
                nc.gpsimd.tensor_scalar(col(S_ST, 64), col(S_SS, 64), 1.0 / DV, EPS, ALU.mult, ALU.add)\
                    .then_inc(s_ost, 1)
                pool.wait_ge(s_ost, b + 1)
                nc.gpsimd.tensor_tensor(col(S_R, 64), col(S_ST, 64), col(N_HALF, 64), ALU.pow).then_inc(s_orms, 1)

            def s_body(b, e):
                s_queries(b, e)
                s_power(b - 3)
            with pool.Fori(0, 2) as i:
                s_body(2 * i + 3, 1)
                s_body(2 * i + 4, 0)
            s_body(NB - 1, 1)
            s_power(NB - 3)
            s_power(NB - 2)

            pool.wait_ge(s_pv, NB - 1)
            for e in range(2):
                for c in range(2):
                    wait(pool, p_zero, 2 * e + c)
                    nc.gpsimd.memset(q_z[(1 - c) * DK:(2 - c) * DK, e, c, :], 0.0).then_inc(p_zero, 1)

            def p_queries(hp, e):
                wait(pool, p_scores, 4 * (2 * hp + e - 1))
                for c in range(2):
                    rows = slice(c * DK, (c + 1) * DK)
                    wait(pool, p_q, 4 * hp + 2 * e + c)
                    nc.gpsimd.tensor_copy(q_z[rows, e, c, :],
                                          qT[rows, bass.ds(2 * hp + e, 1), 0:SEQ].rearrange("p a n -> p (a n)"))\
                        .then_inc(p_q, 1)

            def p_power(hp, e, last_pair):
                h = 2 * hp + e
                pool.wait_ge(p_q, 2 * HEADS if last_pair else 4 * hp + 2 * e + 6)
                pool.wait_ge(p_oss, h + 1)
                settle(pool, hp)
                nc.gpsimd.tensor_scalar(col(P_ST, w=4), col(P_SS + 4 * e, w=4), 1.0 / DV, EPS, ALU.mult, ALU.add)\
                    .then_inc(p_ost, 1)
                pool.wait_ge(p_ost, h + 1)
                nc.gpsimd.tensor_tensor(col(P_R + 4 * e, w=4), col(P_ST, w=4), col(N_HALF, w=4), ALU.pow)\
                    .then_inc(p_orms, 1)

            def p_body(hp, last_pair=False):
                for e in range(2):
                    if not last_pair:
                        p_queries(hp + 1, e)
                    p_power(hp, e, last_pair)
            pool.wait_ge(p_zero, 4)
            p_queries(0, 0)
            p_queries(0, 1)
            pool.wait_ge(p_q, 4)
            s_power(NB - 1)
            pairs(pool, p_body)

            pool.wait_ge(o_lo_done, KT)
            nc.gpsimd.memset(sg_ws[:, :, :], 0.0).then_inc(g_zero, 1)
            pool.wait_ge(sg_loaded, 48)
            nc.gpsimd.affine_select(out=sg_w[:, :, :], in_=sg_w[:, :, :], compare_op=ALU.is_ge, fill=0.0, base=0,
                                    pattern=[[0, GROUPS], [1, P]], channel_multiplier=-1).then_inc(g_wmask, 1)
            pool.wait_ge(sgs_loaded, 16 * NB)
            nc.gpsimd.affine_select(out=sg_ws[:, :, :], in_=sg_ws[:, :, :], compare_op=ALU.is_ge, fill=0.0, base=0,
                                    pattern=[[0, GROUPS], [1, NS]], channel_multiplier=-1).then_inc(g_wmask, 1)
            pool.wait_ge(g_ss, 1)
            nc.gpsimd.tensor_scalar(col(G_ST, w=5), col(G_SS, w=5), 1.0 / D, EPS, ALU.mult, ALU.add)\
                .then_inc(g_st, 1)
            pool.wait_ge(g_st, 1)
            nc.gpsimd.tensor_tensor(col(G_RS, w=5), col(G_ST, w=5), col(N_HALF, w=5), ALU.pow).then_inc(g_rs, 1)
            pool.wait_ge(g_norm, 1)

            def slots(i):
                for u in range(2):
                    n = 2 * i + u
                    wait(pool, g_mix, n - 1)
                    nc.gpsimd.tensor_copy(s_slot[:, u, 0:QT, :], s_nat[:, 0:QT, bass.ds(n * P, P)])\
                        .then_inc(g_slot, 1)
                    nc.gpsimd.tensor_copy(s_slot[0:NS, u, QT, :], s_nat[0:NS, QT, bass.ds(n * P, P)])\
                        .then_inc(g_slot, 1)
            slots(0)
            pool.dma_start(vn_out, s_nat[0:NS, QT, :]).then_inc(stored, 16)
            with pool.Fori(1, 4) as i:
                slots(i)

            norm_pow(1, MEM)
            norm_lo(m_lo, m_hi, MEM, KT)
            def m_body(i):
                for e in range(2):
                    b = 2 * i + e
                    wait(pool, m_scores, b - 1)
                    nc.gpsimd.tensor_copy(view(q_mb[:, e, 0, :], [[2 * 32 + TS, MXH], [32, 2], [1, TS]]),
                                          zmT[:, :, bass.ds(SEQ + b * TS, TS)].rearrange("p (h f) t -> p h f t", f=2))\
                        .then_inc(m_q, 1)

            pool.wait_ge(mm_done, FIRST["zm"])
            nc.gpsimd.memset(q_mb[:, :, :, :], 0.0).then_inc(m_zero, 1)
            pool.wait_ge(m_zero, 1)
            for u in range(2):
                pool.wait_ge(acc_free[u], FIRST["mk"] // 2)
            m_body(0)
            for u in range(2):
                pool.wait_ge(acc_free[u], FIRST["mv"] // 2)
            pool.dma_start(mkT_out.rearrange("(k p) n -> p k n", p=P), kmT[:, :, :]).then_inc(stored, 16)
            pool.wait_ge(nat_done, 3 * KT)
            pool.dma_start(mv_out.rearrange("(m p) n -> p m n", p=P), vm_nat[:, :, :]).then_inc(stored, 16)
            with pool.Fori(1, NB // 2) as i:
                m_body(i)

            norm_pow(2, T)
            norm_pow(3, T)

        @block.tensor
        def _(pe):
            def panel(p, u, x_hi, x_lo, a=None, nk=KT, k0=0, n=HT, nc_=2, start=True, stop=True, tile_ready=None):
                a = u if a is None else a
                pe.wait_ge(w_lo_done, p + 1)
                for k in range(nk):
                    if tile_ready:
                        tile_ready(k)
                    for t, (w, x) in enumerate(((w_hi, x_hi), (w_hi, x_lo), (w_lo, x_hi))):
                        for c in range(nc_):
                            last = nc.tensor.matmul(acc[a][:, c, 0:n], w[:, u, k * P:(k + 1) * P],
                                                    x[:, k0 + k, c * n:(c + 1) * n],
                                                    start=start and k == 0 and t == 0,
                                                    stop=stop and k == nk - 1 and t == 2)
                last.then_inc(mm_done, 1)

            def slot_free(stage, i, u):
                wait(pe, acc_free[u], FIRST[stage] // 2 + i)

            def plain(stage, x_hi, x_lo, first=0, last=4, **kw):
                def body(i):
                    for u in range(2):
                        slot_free(stage, i, u)
                        panel(FIRST[stage] + 2 * i + u, u, x_hi, x_lo, **kw)
                with pe.Fori(first, last) as i:
                    body(i)

            def turn_tile(stage, n, u, count, nt):
                k = (FIRST[stage] + n) // 2 if isinstance(n, int) else FIRST[stage] // 2 + (n - u) // 2
                pe.wait_ge(acc_free[u], k + 1)
                wait(pe, nat_done, count + n - 1)
                for j in range(min(nt, QT)):
                    last = nc.tensor.transpose(bank(4 + u)[:, j * P:(j + 1) * P], turn[:, u, j * P:(j + 1) * P], ident)
                if nt > QT:
                    last = nc.tensor.transpose(bank(6 + u)[0:NS, 0:P], turn[:, u, SEQ:T], ident)
                last.then_inc(turned, 1)

            def turning(stage, x_hi, x_lo, count, nt=QT + 1, **kw):
                def body(i):
                    for u in range(2):
                        slot_free(stage, i, u)
                        panel(FIRST[stage] + 2 * i + u, u, x_hi, x_lo, **kw)
                        if not isinstance(i, int) or u:
                            turn_tile(stage, 2 * i + u - 1, 1 - u, count, nt)
                peeled(pe, 4, body)

            def norm_stats(count, n_cols):
                pe.wait_ge(summed, SUMS[count + 1])
                starts = (0, P, 2 * P, 3 * P, T - P) if n_cols == T else (0, P)
                for j, t0 in enumerate(starts):
                    last = nc.tensor.matmul(bank(4)[:, j:j + 1], ssum[:, t0:t0 + P], cst[:, C_INVD:C_INVD + 1],
                                            start=True, stop=True)
                last.then_inc(stat_mm, 1)

            def norm_bcast(count, n_cols):
                pe.wait_ge(diag_ready, count + 1)
                ones = cst[:, C_ONE:C_ONE + P]
                flat = diag[:, :, :].rearrange("p j n -> p (j n)")
                if n_cols == T:
                    nc.tensor.matmul(bank(5), ones, flat[:, 0:SEQ], start=True, stop=True)
                    last = nc.tensor.matmul(bank(6)[:, 0:NS], ones, flat[:, QT * P + P - NS:QT * P + P],
                                            start=True, stop=True)
                else:
                    last = nc.tensor.matmul(bank(5)[:, 0:MEM], ones, flat[:, 0:MEM], start=True, stop=True)
                last.then_inc(bcast_mm, 1)

            pe.wait_ge(cst_loaded, 32)
            pe.wait_ge(sel_loaded, 16)
            for half, b in enumerate((7, 3)):
                last = nc.tensor.matmul(bank(b)[0:HEADS, 0:HREV], par[0:BUCKETS + 1, G_REL:G_REL + HEADS],
                                        b_sel[:, half * HREV:(half + 1) * HREV], start=True, stop=True)
            last.then_inc(line_mm, 1)
            norm_stats(0, T)
            norm_bcast(0, T)
            pe.wait_ge(line_ready, 2)
            pe.wait_ge(lam_neg, 1)
            nc.tensor.matmul(bank(7)[:, LAM_AT:LAM_AT + 1], cst[0:1, C_ONE:C_ONE + P], lam_w[0:1, 2 * DK + 5:2 * DK + 6],
                             start=True, stop=True).then_inc(lam_mm, 1)

            def h_tile(k):
                pe.wait_ge(n_lo if k % 2 == 0 else n_lo_odd, k // 2 + 1)
            panel(0, 0, h_hi, h_lo, tile_ready=h_tile)
            panel(1, 1, h_hi, h_lo)
            plain("q", h_hi, h_lo, 1, 4)
            plain("k", h_hi, h_lo)
            turning("v", h_hi, h_lo, 0)

            pe.wait_ge(acc_free[0], FIRST["da_branch"] // 2)
            pe.wait_ge(v_zero, 2)

            def s_score(b, i, e):
                pe.wait_ge(k_loaded[e], 16 * PAGES * (i + 1))
                pe.wait_ge(s_q, 3 * (b + 1))
                wait(pe, s_logit, b)
                for h in range(HEADS):
                    for c in range(2):
                        last = nc.tensor.matmul(acc[0][:, c, 0:HK], q_blk[:, h, :], k_slot[e][:, h, c * HK:(c + 1) * HK],
                                                start=h == 0, stop=h == HEADS - 1)
                last.then_inc(s_scores, 1)

            def s_combine(b, e):
                pe.wait_ge(s_coef, b + 1)
                wait(pe, s_aT, b)
                for j in range(PAGES):
                    nc.tensor.matmul(bank(2)[:, j * 64:(j + 1) * 64], logit_s[:, e, j * P:(j + 1) * P], coef_s[:, :],
                                     start=True, stop=True)
                nc.tensor.matmul(bank(3)[0:TS, 0:64], logit_s[:, e, PAST:KEYS], coef_s[:, :], start=True, stop=True)\
                    .then_inc(s_comb, 1)

            def s_values(b, pg=v_pg, loaded=v_loaded, loads=None):
                pe.wait_ge(s_aT, b + 1)
                pe.wait_ge(loaded, 16 * PAGES * (b + 1 if loads is None else loads))
                wait(pe, s_masked, b)
                for half in range(2):
                    cols = slice(half * 512, (half + 1) * 512)
                    for j in range(PAGES + 1):
                        if half == 0 and j == PAGES:
                            pe.wait_ge(v_new_loaded, 16 * (b + 1))
                            settle(pe, b)
                        v = pg[:, j, cols] if j < PAGES else v_new[:, cols]
                        last = nc.tensor.matmul(bank(4 + half)[0:64, :], aT_s[:, j * 64:(j + 1) * 64], v,
                                                start=j == 0, stop=j == PAGES)
                last.then_inc(s_pv, 1)

            def s_turn(b):
                pe.wait_ge(s_onorm, b + 1)
                wait(pe, s_oout, b)
                settle(pe, b)
                nc.tensor.transpose(bank(6)[:, 0:64], o_s[:, 1, :], cst[0:64, C_ID:C_ID + 64]).then_inc(s_oT, 1)

            def s_body(i):
                for e in range(2):
                    b = 2 * i + e
                    s_score(b, i, e)
                    if isinstance(b, int) and b == 0:
                        turn_tile("v", KT - 1, 1, 0, QT + 1)
                        pe.wait_ge(nat_done, KT)
                    if not isinstance(b, int) or b >= 3:
                        s_turn(b - 3)
                    if not isinstance(b, int) or b >= 2:
                        s_values(b - 2)
                    if not isinstance(b, int) or b >= 1:
                        s_combine(b - 1, 1 - e)
            peeled(pe, NB // 2, s_body, 2)
            s_values(NB - 2, v_late, v_late_loaded, 1)
            s_combine(NB - 1, 1)
            s_turn(NB - 3)
            s_values(NB - 1, loads=NB - 1)
            s_turn(NB - 2)

            pe.wait_ge(p_zero, 4)
            pe.wait_ge(s_masked, NB)

            def turn_output(h, e):
                pe.wait_ge(p_onorm, h + 1)
                for i in range(QT):
                    last = nc.tensor.transpose(bank(2 + e)[:, i * P:(i + 1) * P], o_p[:, e, i * DV:(i + 1) * DV], ident)
                last.then_inc(p_oT, 1)

            def p_body(hp0, last_pair=False):
                def score(n):
                    hp, n = hp0 + n // 8, n % 8
                    m, e, i = n % 2, n // 4, TILE_ORDER[n % 4]
                    w = (i + 1) * P
                    pe.wait_ge(p_q, 2 * (2 * hp + e + 1))
                    wait(pe, p_logit, 8 * hp + n - 1)
                    for c in range(2):
                        last = nc.tensor.matmul(bank(4 + 2 * m + c)[:, 0:w], q_z[:, e, c, i * P:(i + 1) * P],
                                                kT[:, bass.ds(2 * hp + e, 1), 0:w].rearrange("p a n -> p (a n)"),
                                                start=True, stop=True)
                    last.then_inc(p_scores, 1)

                def turn_probs(n):
                    hp = hp0
                    m, i = n % 2, TILE_ORDER[n % 4]
                    pe.wait_ge(p_a, 8 * hp + n + 1)
                    wait(pe, p_aT, 8 * hp + n - 1)
                    for j in range(i + 1):
                        last = nc.tensor.transpose(bank(m)[:, j * P:(j + 1) * P], a_p[:, m, j * P:(j + 1) * P], ident)
                    last.then_inc(p_turn, 1)

                def values(n):
                    hp, n = hp0 + n // 8, n % 8
                    m, e, i = n % 2, n // 4, TILE_ORDER[n % 4]
                    pe.wait_ge(p_aT, 8 * hp + n + 1)
                    if n % 4 == 0:
                        wait(pe, p_oout, 2 * hp + e - 1)
                    for j in range(i + 1):
                        last = nc.tensor.matmul(bank(2 + e)[:, i * DV:(i + 1) * DV], aT_p[:, m, j * P:(j + 1) * P],
                                                v_nat[:, j, bass.ds((2 * hp + e) * DV, DV)],
                                                start=j == 0, stop=j == i)
                    last.then_inc(p_pv, 1)

                def turn_out(e, hp):
                    turn_output(2 * hp + e, e)

                first_pair = isinstance(hp0, int) and hp0 == 0
                if first_pair:
                    score(0)
                    s_turn(NB - 1)
                    pe.wait_ge(s_oout, NB)
                    score(1)
                for n in range(8):
                    if n < 6 or not last_pair:
                        score(n + 2)
                    turn_probs(n)
                    if n > 0 or not first_pair:
                        values(n - 1)
                    if n == 3 and not first_pair:
                        turn_out(1, hp0 - 1)
                    if n == 7:
                        turn_out(0, hp0)
                if last_pair:
                    values(7)
            pairs(pe, p_body)

            def branch(stage, split, before_output=None):
                def o_tile(k):
                    pe.wait_ge(o_lo_done, split - KT + k + 1)

                def body(i):
                    slot_free(stage, i, 0)
                    panel(FIRST[stage] + 2 * i, 0, h_hi, h_lo)
                    if before_output and isinstance(i, int):
                        before_output()
                    slot_free(stage, i, 1)
                    panel(FIRST[stage] + 2 * i + 1, 1, o_hi, o_lo, tile_ready=o_tile if isinstance(i, int) else None)
                peeled(pe, KT, body)

            def last_head():
                turn_output(HEADS - 1, 1)
                pe.wait_ge(p_oout, HEADS)
            branch("da_branch", KT, last_head)

            turning("s", h_hi, h_lo, KT)

            def mix(n, u):
                pe.wait_ge(g_slot, 2 * (n + 1))
                wait(pe, g_bias, n - 1)
                group = bass.ds(n, 1)
                for j in range(QT):
                    nc.tensor.matmul(bank(4 + u)[:, j * P:(j + 1) * P], s_slot[:, u, j, :],
                                     sg_w[:, group, :].rearrange("p a n -> p (a n)"), start=True, stop=True)
                nc.tensor.matmul(bank(6 + u)[:, 0:NS], s_slot[0:NS, u, QT, :],
                                 sg_ws[:, group, :].rearrange("p a n -> p (a n)"), start=True, stop=True)\
                    .then_inc(g_mix, 1)

            def u_body(i):
                for u in range(2):
                    slot_free("u", i, u)
                    panel(FIRST["u"] + 2 * i + u, u, h_hi, h_lo)
                    if not isinstance(i, int) or i and u:
                        mix(2 * i + u - 3, 1 - u)
                    elif i == 0 and u == 0:
                        turn_tile("s", KT - 1, 1, KT, QT + 1)
                    elif i == 0:
                        pe.wait_ge(nat_done, 2 * KT)
                        pe.wait_ge(g_wmask, 2)
            peeled(pe, 4, u_body, 2)
            for n in range(KT - 3, KT):
                mix(n, n % 2)
            branch("sg_branch", 2 * KT)

            plain("zm", h_hi, h_lo, 0, 1)
            norm_stats(1, MEM)
            plain("zm", h_hi, h_lo, 1, 2)
            norm_bcast(1, MEM)
            plain("zm", h_hi, h_lo, 2, 4)
            pe.wait_ge(n_lo, KT)
            pe.wait_ge(n_lo_odd, KT)
            plain("mk", m_hi, m_lo, n=MEM, nc_=1)
            turning("mv", m_hi, m_lo, 2 * KT, MT, n=MEM, nc_=1)
            pe.wait_ge(nat_done, 3 * KT - 1)

            def m_score(b, e, i):
                pe.wait_ge(km_loaded[e], 16 * i + 16)
                pe.wait_ge(m_q, b + 1)
                wait(pe, m_exp, b - 1)
                for f in range(KT):
                    last = nc.tensor.matmul(bank(4 + e)[0:32, 0:MEM], q_mb[:, e, f, :], km_pg[:, e, f, :],
                                            start=f == 0, stop=f == KT - 1)
                last.then_inc(m_scores, 1)

            def m_turn_p(b, e):
                pe.wait_ge(m_p, b + 1)
                wait(pe, m_pT, b)
                settle(pe, b)
                for m in range(MT):
                    last = nc.tensor.transpose(bank(6)[:, m * 32:(m + 1) * 32], p_mb[:, e, m * P:(m + 1) * P],
                                               cst[0:32, C_ID:C_ID + 32])
                last.then_inc(m_turn, 1)

            def m_values(b, e, i):
                pe.wait_ge(m_pT, b + 1)
                pe.wait_ge(vm_loaded[e], 16 * i + 16)
                wait(pe, m_masked, b)
                for half in range(2):
                    for m in range(MT):
                        last = nc.tensor.matmul(bank(half)[0:32, :], pT_mb[:, e, m * 32:(m + 1) * 32],
                                                vm_pg[:, e, m, half * 512:(half + 1) * 512], start=m == 0, stop=m == 1)
                last.then_inc(m_pv, 1)

            def m_turn_o(b, e):
                pe.wait_ge(m_o, b + 1)
                wait(pe, m_oout, b)
                settle(pe, b)
                for f in range(2):
                    last = nc.tensor.transpose(bank(7)[:, f * 32:(f + 1) * 32], o_m[:, e, f * P:(f + 1) * P],
                                               cst[0:32, C_ID:C_ID + 32])
                last.then_inc(m_oT, 1)

            def m_body(i):
                for e in range(2):
                    b = 2 * i + e
                    m_score(b, e, i)
                    if isinstance(b, int) and b == 0:
                        turn_tile("mv", KT - 1, 1, 2 * KT, MT)
                        all_evacuated(pe, "mx_branch")
                        pe.wait_ge(nat_done, 3 * KT)
                    if not isinstance(i, int):
                        m_turn_o(b - 2, e)
                    if not isinstance(i, int) or e:
                        m_values(b - 1, 1 - e, i if e else i - 1)
                    m_turn_p(b, e)
            peeled(pe, NB // 2, m_body)
            def c_score(h):
                wait(pe, c_exp, h - 1)
                for i in range(QT):
                    for f in range(2):
                        last = nc.tensor.matmul(score_banks(h)[:, i // 2, (i % 2) * MEM:(i % 2 + 1) * MEM],
                                                zmT[:, 2 * h + f, i * P:(i + 1) * P], kmT[:, 2 * h + f, :],
                                                start=f == 0, stop=f == 1)
                last.then_inc(c_scores, 1)

            def c_turn_p(h):
                pe.wait_ge(c_p, h + 1)
                wait(pe, c_pT, h)
                for m in range(MT):
                    for i in range(QT):
                        last = nc.tensor.transpose(bank(6 + m)[:, i * P:(i + 1) * P], p_m[:, h % 2, i, m * P:(m + 1) * P], ident)
                last.then_inc(c_turn, 1)

            def c_values(h):
                pe.wait_ge(c_pT, h + 1)
                wait(pe, c_oout, h)
                if h == MXH - 1:
                    pe.wait_ge(c_exp, h)
                for f in range(2):
                    for m in range(MT):
                        last = nc.tensor.matmul(bank(pv_bank(h) + f), vm_nat[:, m, h * MXD + f * P:h * MXD + (f + 1) * P],
                                                pT_m[:, m, :], start=m == 0, stop=m == 1)
                last.then_inc(c_pv, 1)

            m_turn_o(NB - 2, 0)
            m_values(NB - 1, 1, NB // 2 - 1)
            c_score(0)
            m_turn_o(NB - 1, 1)
            pe.wait_ge(m_exp, NB)
            c_score(1)
            pe.wait_ge(m_oout, NB)
            pe.wait_ge(m_masked, NB)
            c_turn_p(0)
            for h in range(1, MXH):
                if h < MXH - 1:
                    c_score(h + 1)
                c_values(h - 1)
                c_turn_p(h)
            pe.wait_ge(c_oout, MXH - 1)

            def last_values():
                c_values(MXH - 1)
                pe.wait_ge(c_oout, MXH)
            branch("mx_branch", 3 * KT, last_values)

            def merged_tile(k):
                pe.wait_ge(o_lo_done, 3 * KT + k + 1)
            slot_free("w_out", 0, 0)
            panel(FIRST["w_out"], 0, m2_hi, m2_lo, tile_ready=merged_tile)
            slot_free("w_out", 0, 1)
            panel(FIRST["w_out"] + 1, 1, m2_hi, m2_lo)
            plain("w_out", m2_hi, m2_lo, 1, 4)

            def g_tile(k):
                pe.wait_ge(n_lo, KT + k + 1)
            slot_free("up", 0, 0)
            panel(FIRST["up"], 0, h_hi, h_lo, tile_ready=g_tile)
            norm_stats(2, T)
            slot_free("up", 0, 1)
            panel(FIRST["up"] + 1, 1, h_hi, h_lo)
            norm_bcast(2, T)
            with pe.Fori(1, FT) as i:
                for u in range(2):
                    slot_free("up", i, u)
                    panel(FIRST["up"] + 2 * i + u, u, h_hi, h_lo)
            def down_body(i):
                for f in range(2):
                    wait(pe, down_free[f], i)
                    k0 = 0
                    for c, nk in enumerate(DOWN_K):
                        q = 3 * f + c
                        if isinstance(i, int):
                            if c == 0:
                                pe.wait_ge(acc_free[f], FIRST["down"] // 2)
                            if f == 0:
                                pe.wait_ge(ffn_lo, k0 + nk)
                        panel(FIRST["down"] + 6 * i + q, q % 2, g_hi, g_lo, a=f, nk=nk, k0=k0,
                              start=c == 0, stop=c == 2)
                        k0 += nk
            peeled(pe, 4, down_body)
            norm_stats(3, T)
            norm_bcast(3, T)


def bucket_selection():
    import math
    import numpy as np
    out = np.zeros((BUCKETS + 1, REV), np.float32)
    exact = BUCKETS // 2
    for y in range(REV):
        d = KEYS - 1 - y
        n = max(d, 0)
        if n < exact:
            b = n
        else:
            ratio = np.log(np.float32(n) / np.float32(exact)) / np.float32(math.log(128 / exact))
            b = min(exact + int(np.float32(ratio) * np.float32(BUCKETS - exact)), BUCKETS - 1)
        out[b, y] = 1.0
        if d < 0:
            out[BUCKETS, y] = NEG
    return out


def constants():
    import numpy as np
    c = np.zeros((P, C_END), np.float32)
    c[:, C_ID:C_ID + P] = np.eye(P)
    c[:, C_ONE:C_ONE + P] = 1.0
    for h in range(HEADS):
        for m in range(2):
            for t in range(TS):
                c[h * 16 + m * 8 + t, C_COMB + h * 8 + t] = 1.0
                c[h * 16 + m * 8 + t, C_C1] = float(m)
        c[h * 8:(h + 1) * 8, C_M8 + h] = 1.0
    for h in range(MXH):
        c[h * 8:(h + 1) * 8, C_M4 + h] = 1.0
    c[:, C_INVD] = 1.0 / D
    return c


def weight_stream(w_in, w_mem_kv, w_branch, w_out, w_up, w_down):
    import numpy as np

    def panels(w, start=0, n=KT):
        part = w[:, start:start + n * P]
        return part.reshape(KT, P, n, P).transpose(2, 1, 0, 3).reshape(n, P, D)

    def paired(a, b):
        return np.stack([a, b], 1).reshape(2 * a.shape[0], P, D)

    gates = 6 * D
    branches = [paired(panels(w_in, gates + r * D), panels(w_branch[r * D:(r + 1) * D])) for r in range(3)]
    down = w_down.reshape(FT, P, KT, P).transpose(2, 1, 0, 3)
    down = np.concatenate([down, np.zeros((KT, P, 3 * KT - FT, P), w_down.dtype)], 2)
    down = down.reshape(KT, P, 3, D).transpose(0, 2, 1, 3).reshape(3 * KT, P, D)
    return np.ascontiguousarray(np.concatenate([
        panels(w_in, 0, 24), branches[0], panels(w_in, 4 * D), panels(w_in, 3 * D), branches[1],
        panels(w_in, 5 * D), panels(w_mem_kv, 0, 16), branches[2], panels(w_out),
        paired(panels(w_up, 0, FT), panels(w_up, DFF, FT)), down]))


def kernel(x_prompt, x_sample, mem_prompt, cache_da_k, cache_da_v, cache_mem_k, cache_mem_v, page_table,
           g_attn, w_in, da_lam, da_subln, rel_bias, sg_norm, sg_w, sg_b, g_mem, w_mem_kv, w_branch, w_out,
           g_ffn, w_up, w_down, g_final):
    import numpy as np
    import concourse.bacc as bacc
    from concourse.bass_utils import run_bass_kernel_spmd

    def host(a):
        return np.asarray(a)

    params = np.zeros((P, G_END), np.float32)
    for at, g in ((G_ATTN, g_attn), (G_MEM, g_mem), (G_FFN, g_ffn), (G_FINAL, g_final)):
        params[:, at:at + KT] = host(g).reshape(KT, P).T
    params[:, G_SUB] = host(da_subln)[0]
    params[0:BUCKETS, G_REL:G_REL + HEADS] = host(rel_bias)
    params[BUCKETS, G_REL:G_REL + HEADS] = 1.0
    params[0, G_LAM:G_END] = host(da_lam).reshape(-1)

    n_pool = cache_da_k.shape[1]
    arrays = {
        "xT": np.concatenate([host(x_prompt)[0], host(x_sample).reshape(NS, D)]).T,
        "memT": host(mem_prompt)[0].T,
        "w_stream": weight_stream(host(w_in)[0], host(w_mem_kv)[0], host(w_branch)[0], host(w_out)[0],
                                  host(w_up)[0], host(w_down)[0]),
        "page_table": host(page_table).reshape(1, -1),
        "cache_k": host(cache_da_k)[0].transpose(0, 3, 2, 1).reshape(n_pool, P, HEADS * PAGE),
        "cache_v": host(cache_da_v)[0].reshape(n_pool, PAGE, D),
        "mem_k": host(cache_mem_k)[0].reshape(NB, MEM, KT, P).transpose(0, 3, 2, 1).reshape(NB, P, KT * MEM),
        "mem_v": host(cache_mem_v)[0].reshape(NB, MEM, D),
        "consts": constants(),
        "bias_select": bucket_selection(),
        "params": params,
        "sg_norm": host(sg_norm),
        "sg_bias": host(sg_b)[0],
        "sg_wT": host(sg_w)[0].transpose(2, 0, 1),
    }
    arrays = {k: np.ascontiguousarray(a) for k, a in arrays.items()}
    outputs = {"yT": (D, T), "kT_out": (D, T), "v_out": (SEQ, D), "vs_out": (NS, D), "mkT_out": (D, MEM),
               "mv_out": (MEM, D), "vn_out": (NS, D)}

    nc = bacc.Bacc("TRN2", target_bir_lowering=False, num_devices=1)
    args = [nc.dram_tensor(k, a.shape, mybir.dt.from_np(a.dtype), kind="ExternalInput").ap()
            for k, a in arrays.items()]
    args += [nc.dram_tensor(k, shape, F32, kind="ExternalOutput").ap() for k, shape in outputs.items()]
    decoder_layer(nc, *args)
    got = run_bass_kernel_spmd(nc, [arrays], core_ids=[0]).results[0]

    y, k = got["yT"].T, got["kT_out"].T
    return (y[0:SEQ].reshape(1, SEQ, D), y[SEQ:T].reshape(NB, TS, D),
            k[0:SEQ].reshape(1, 1, SEQ, HEADS, 2 * DK), got["v_out"].reshape(1, 1, SEQ, HEADS, DV),
            k[SEQ:T].reshape(1, NB, TS, HEADS, 2 * DK), got["vs_out"].reshape(1, NB, TS, HEADS, DV),
            got["mkT_out"].T.reshape(1, 1, MEM, MXH, MXD), got["mv_out"].reshape(1, 1, MEM, MXH, MXD),
            got["vn_out"].reshape(1, NB, TS, D))
```
